# Optimizing a Trainium2 kernel written in Bass

```python
import math
import jax, jax.numpy as jnp
from jax import lax
import numpy as np

D_MODEL = 1024
BATCH = 1
SEQ = 1024
DEPTH = 1
DEC_BATCH = 8
DEC_SEQ = 1
PAST_LEN = 8192
PAGE_SIZE = 128

MIX_WIDTH = D_MODEL
LRU_WIDTH = (3 * MIX_WIDTH) // 8
LRU_HEADS = 6
LRU_HEAD_DIM = LRU_WIDTH // LRU_HEADS
CONV_WIDTH = 4
LRU_C = 8.0
MLSTM_WIDTH = (3 * MIX_WIDTH) // 8
MLSTM_HEADS = 4
MLSTM_HEAD_DIM = MLSTM_WIDTH // MLSTM_HEADS
MLSTM_CHUNK = 128
POOL_WIDTH = MIX_WIDTH - LRU_WIDTH - MLSTM_WIDTH
POOL_WINDOWS = (2, 4, 8, 16)
POOL_GROUPS = 4
POOL_GROUP_DIM = POOL_WIDTH // POOL_GROUPS
POOL_BUF = 15
D_FF = 4 * D_MODEL
EPS = 1e-6
IN_COLS = 2 * LRU_WIDTH + 4 * MLSTM_WIDTH + 2 * MLSTM_HEADS + POOL_WIDTH

kernel_name = "hybrid_rglru_mlstm_pool_decode_step"

def _in_splits():
    widths = (LRU_WIDTH, LRU_WIDTH, MLSTM_WIDTH, MLSTM_WIDTH, MLSTM_WIDTH, MLSTM_WIDTH,
              MLSTM_HEADS, MLSTM_HEADS, POOL_WIDTH)
    return tuple(int(s) for s in np.cumsum(widths)[:-1])

def rmsnorm(x, g):
    xf = x.astype(jnp.float32)
    y = xf * lax.rsqrt(jnp.mean(xf * xf, axis=-1, keepdims=True) + EPS)
    return (y * g).astype(x.dtype)

def causal_dwconv(x, buf, w, b):
    L = x.shape[1]
    xp = jnp.concatenate([buf.astype(x.dtype), x], axis=1)
    y = b
    for j in range(CONV_WIDTH):
        y = y + w[j] * xp[:, j:j + L]
    return y, xp[:, L:]

def rglru(x, h0, w_a, b_a, w_x, b_x, lam, is_start):
    B, L, W = x.shape
    xf = x.astype(jnp.float32)
    xh = xf.reshape(B, L, LRU_HEADS, LRU_HEAD_DIM)
    r = jax.nn.sigmoid(jnp.einsum('blhi,hij->blhj', xh, w_a) + b_a).reshape(B, L, W)
    i = jax.nn.sigmoid(jnp.einsum('blhi,hij->blhj', xh, w_x) + b_x).reshape(B, L, W)
    log_a = LRU_C * r * jax.nn.log_sigmoid(lam.astype(jnp.float32))
    a = jnp.exp(log_a)
    mult = jnp.sqrt(-jnp.expm1(2.0 * log_a))
    if is_start:
        mult = mult.at[:, 0].set(1.0)
    bterm = mult * i * xf
    bterm = bterm.at[:, 0].add(a[:, 0] * h0.astype(jnp.float32))

    def combine(lhs, rhs):
        a1, b1 = lhs
        a2, b2 = rhs
        return a1 * a2, a2 * b1 + b2

    _, h = lax.associative_scan(combine, (a, bterm), axis=1)
    return h, h[:, -1]

def mlstm(q, k, v, ig, fg, C0, n0, m0):
    B, L, H, d = q.shape
    Lc = MLSTM_CHUNK if L % MLSTM_CHUNK == 0 else L
    NC = L // Lc
    f32 = jnp.float32

    def chunks(t):
        return t.astype(f32).reshape(B, NC, Lc, H, d).transpose(1, 0, 3, 2, 4)

    def gchunks(t):
        return t.astype(f32).reshape(B, NC, Lc, H).transpose(1, 0, 3, 2)

    qc = chunks(q)
    kc = chunks(k) / math.sqrt(d)
    vc = chunks(v)
    ic = gchunks(ig)
    lfc = gchunks(jax.nn.log_sigmoid(fg.astype(f32)))
    mask = jnp.tril(jnp.ones((Lc, Lc), dtype=bool))

    def step(carry, inp):
        C, n, m = carry
        qb, kb, vb, ib, lfb = inp
        bcum = jnp.cumsum(lfb, axis=-1)
        D = bcum[..., :, None] - bcum[..., None, :] + ib[..., None, :]
        D = jnp.where(mask, D, -jnp.inf)
        g = bcum + m[..., None]
        m_t = jnp.maximum(g, jnp.max(D, axis=-1))
        inter = jnp.exp(g - m_t)
        S = jnp.einsum('bhtd,bhsd->bhts', qb, kb) * jnp.exp(D - m_t[..., None])
        num = jnp.einsum('bhts,bhsd->bhtd', S, vb) + inter[..., None] * jnp.einsum('bhvk,bhtk->bhtv', C, qb)
        den = jnp.sum(S, axis=-1) + inter * jnp.einsum('bhk,bhtk->bht', n, qb)
        h = num / jnp.maximum(jnp.abs(den), jnp.exp(-m_t))[..., None]
        m_new = m_t[..., -1]
        decay = jnp.exp(bcum[..., -1] + m - m_new)
        w = jnp.exp(bcum[..., -1:] - bcum + ib - m_new[..., None])
        C_new = decay[..., None, None] * C + jnp.einsum('bhs,bhsv,bhsk->bhvk', w, vb, kb)
        n_new = decay[..., None] * n + jnp.einsum('bhs,bhsk->bhk', w, kb)
        return (C_new, n_new, m_new), h

    (C1, n1, m1), hs = lax.scan(step, (C0.astype(f32), n0.astype(f32), m0.astype(f32)),
                                (qc, kc, vc, ic, lfc))
    h = hs.transpose(1, 0, 3, 2, 4).reshape(B, L, H, d)
    return h, C1, n1, m1

def pool_mix(u, buf, pool_w, pool_scale, start_pos):
    B, L, C = u.shape
    up = jnp.concatenate([buf.astype(u.dtype), u], axis=1)
    cs = jnp.concatenate([jnp.zeros((B, 1, C), jnp.float32),
                          jnp.cumsum(up.astype(jnp.float32), axis=1)], axis=1)
    pos = start_pos + jnp.arange(L)
    outs = []
    for gi, win in enumerate(POOL_WINDOWS):
        sl = slice(gi * POOL_GROUP_DIM, (gi + 1) * POOL_GROUP_DIM)
        cg = cs[..., sl]
        s = cg[:, POOL_BUF + 1:POOL_BUF + 1 + L] - cg[:, POOL_BUF + 1 - win:POOL_BUF + 1 - win + L]
        cnt = jnp.minimum(pos + 1, win).astype(jnp.float32)
        diff = s / cnt[None, :, None] - u[..., sl].astype(jnp.float32)
        outs.append(jnp.einsum('blc,cd->bld', diff, pool_w[gi]) * pool_scale[gi])
    return jnp.concatenate(outs, axis=-1).astype(u.dtype), up[:, L:]

def layer(x, c, start_pos, lru_h0, conv_buf, C0, n0, m0, pool_buf,
          norm1_g, norm2_g, w_ada, b_ada, w_in, conv_w, conv_b, lru_wa, lru_ba, lru_wx, lru_bx,
          lru_lam, mlstm_bi, mlstm_bf, mlstm_norm_g, pool_w, pool_scale, w_out, w_ff1, w_ff2):
    B, L, _ = x.shape
    mod = jax.nn.silu(c) @ w_ada + b_ada
    sh1, sc1, gt1, sh2, sc2, gt2 = jnp.split(mod[:, None, :], 6, axis=-1)
    h = rmsnorm(x, norm1_g) * (1.0 + sc1) + sh1
    proj = h @ w_in
    xr, gr, q, k, v, o, ig, fg, u = jnp.split(proj, _in_splits(), axis=-1)
    xc, conv_new = causal_dwconv(xr, conv_buf, conv_w, conv_b)
    hseq, h_last = rglru(xc, lru_h0, lru_wa, lru_ba, lru_wx, lru_bx, lru_lam, start_pos == 0)
    y_a = hseq.astype(x.dtype) * jax.nn.gelu(gr)
    hm, C1, n1, m1 = mlstm(q.reshape(B, L, MLSTM_HEADS, MLSTM_HEAD_DIM),
                           k.reshape(B, L, MLSTM_HEADS, MLSTM_HEAD_DIM),
                           v.reshape(B, L, MLSTM_HEADS, MLSTM_HEAD_DIM),
                           ig + mlstm_bi, fg + mlstm_bf, C0, n0, m0)
    hm = rmsnorm(hm, mlstm_norm_g).astype(x.dtype)
    y_b = jax.nn.sigmoid(o) * hm.reshape(B, L, MLSTM_WIDTH)
    y_c, pool_new = pool_mix(u, pool_buf, pool_w, pool_scale, start_pos)
    mix = jnp.concatenate([y_a, y_b, y_c], axis=-1) @ w_out
    x = x + gt1 * mix
    h2 = rmsnorm(x, norm2_g) * (1.0 + sc2) + sh2
    x = x + gt2 * (jnp.square(jax.nn.relu(h2 @ w_ff1)) @ w_ff2)
    return x, (h_last, conv_new, C1, n1, m1, pool_new)

def setup_inputs(seed: int = 0) -> dict:
    key = jax.random.key(seed)
    ks = jax.random.split(key, 40)
    nrm = lambda i, shape, s: jax.random.normal(ks[i], shape, jnp.float32) * s
    a0 = jax.random.uniform(ks[20], (DEPTH, LRU_WIDTH), jnp.float32, 0.9, 0.999)
    return {
        "x_prompt": nrm(0, (BATCH, SEQ, D_MODEL), 1.0),
        "x_sample": nrm(1, (DEC_BATCH, DEC_SEQ, D_MODEL), 1.0),
        "state_lru_h": nrm(2, (DEPTH, DEC_BATCH, LRU_WIDTH), 0.5),
        "state_lru_conv": nrm(3, (DEPTH, DEC_BATCH, CONV_WIDTH - 1, LRU_WIDTH), 1.0),
        "state_mlstm_C": nrm(4, (DEPTH, DEC_BATCH, MLSTM_HEADS, MLSTM_HEAD_DIM, MLSTM_HEAD_DIM), 0.1),
        "state_mlstm_n": nrm(5, (DEPTH, DEC_BATCH, MLSTM_HEADS, MLSTM_HEAD_DIM), 0.3),
        "state_mlstm_m": jax.random.uniform(ks[6], (DEPTH, DEC_BATCH, MLSTM_HEADS), jnp.float32, 0.0, 3.0),
        "state_pool": nrm(7, (DEPTH, DEC_BATCH, POOL_BUF, POOL_WIDTH), 1.0),
        "c_prompt": nrm(8, (BATCH, D_MODEL), 1.0),
        "c_sample": nrm(9, (DEC_BATCH, D_MODEL), 1.0),
        "norm1_g": 1.0 + nrm(10, (DEPTH, D_MODEL), 0.02),
        "norm2_g": 1.0 + nrm(11, (DEPTH, D_MODEL), 0.02),
        "w_ada": nrm(12, (DEPTH, D_MODEL, 6 * D_MODEL), 0.5 * D_MODEL ** -0.5),
        "b_ada": nrm(13, (DEPTH, 6 * D_MODEL), 0.02),
        "w_in": nrm(14, (DEPTH, D_MODEL, IN_COLS), D_MODEL ** -0.5),
        "conv_w": nrm(15, (DEPTH, CONV_WIDTH, LRU_WIDTH), CONV_WIDTH ** -0.5),
        "conv_b": nrm(16, (DEPTH, LRU_WIDTH), 0.02),
        "lru_wa": nrm(17, (DEPTH, LRU_HEADS, LRU_HEAD_DIM, LRU_HEAD_DIM), LRU_HEAD_DIM ** -0.5),
        "lru_ba": nrm(18, (DEPTH, LRU_HEADS, LRU_HEAD_DIM), 0.02),
        "lru_wx": nrm(19, (DEPTH, LRU_HEADS, LRU_HEAD_DIM, LRU_HEAD_DIM), LRU_HEAD_DIM ** -0.5),
        "lru_bx": nrm(21, (DEPTH, LRU_HEADS, LRU_HEAD_DIM), 0.02),
        "lru_lam": jnp.log(a0) - jnp.log1p(-a0),
        "mlstm_bi": nrm(22, (DEPTH, MLSTM_HEADS), 0.1),
        "mlstm_bf": jnp.linspace(3.0, 6.0, MLSTM_HEADS, dtype=jnp.float32)[None, :] + nrm(23, (DEPTH, MLSTM_HEADS), 0.1),
        "mlstm_norm_g": 1.0 + nrm(24, (DEPTH, MLSTM_HEADS, MLSTM_HEAD_DIM), 0.02),
        "pool_w": nrm(25, (DEPTH, POOL_GROUPS, POOL_GROUP_DIM, POOL_GROUP_DIM), POOL_GROUP_DIM ** -0.5),
        "pool_scale": 0.5 + nrm(26, (DEPTH, POOL_GROUPS, POOL_GROUP_DIM), 0.05),
        "w_out": nrm(27, (DEPTH, MIX_WIDTH, D_MODEL), MIX_WIDTH ** -0.5),
        "w_ff1": nrm(28, (DEPTH, D_MODEL, D_FF), D_MODEL ** -0.5),
        "w_ff2": nrm(29, (DEPTH, D_FF, D_MODEL), D_FF ** -0.5),
        "final_g": 1.0 + nrm(30, (D_MODEL,), 0.02),
    }

def reference(x_prompt, x_sample, state_lru_h, state_lru_conv, state_mlstm_C, state_mlstm_n,
              state_mlstm_m, state_pool, c_prompt, c_sample, norm1_g, norm2_g, w_ada, b_ada, w_in,
              conv_w, conv_b, lru_wa, lru_ba, lru_wx, lru_bx, lru_lam, mlstm_bi, mlstm_bf,
              mlstm_norm_g, pool_w, pool_scale, w_out, w_ff1, w_ff2, final_g):
    Bp = x_prompt.shape[0]
    f32 = jnp.float32
    xp, xs = x_prompt, x_sample
    p_states, s_states = [], []
    for l in range(DEPTH):
        params = (norm1_g[l], norm2_g[l], w_ada[l], b_ada[l], w_in[l], conv_w[l], conv_b[l],
                  lru_wa[l], lru_ba[l], lru_wx[l], lru_bx[l], lru_lam[l], mlstm_bi[l], mlstm_bf[l],
                  mlstm_norm_g[l], pool_w[l], pool_scale[l], w_out[l], w_ff1[l], w_ff2[l])
        xp, st_p = layer(xp, c_prompt, 0,
                         jnp.zeros((Bp, LRU_WIDTH), f32),
                         jnp.zeros((Bp, CONV_WIDTH - 1, LRU_WIDTH), xp.dtype),
                         jnp.zeros((Bp, MLSTM_HEADS, MLSTM_HEAD_DIM, MLSTM_HEAD_DIM), f32),
                         jnp.zeros((Bp, MLSTM_HEADS, MLSTM_HEAD_DIM), f32),
                         jnp.zeros((Bp, MLSTM_HEADS), f32),
                         jnp.zeros((Bp, POOL_BUF, POOL_WIDTH), xp.dtype),
                         *params)
        xs, st_s = layer(xs, c_sample, PAST_LEN, state_lru_h[l], state_lru_conv[l], state_mlstm_C[l],
                         state_mlstm_n[l], state_mlstm_m[l], state_pool[l], *params)
        p_states.append(st_p)
        s_states.append(st_s)
    y_prompt = rmsnorm(xp, final_g)
    y_sample = rmsnorm(xs, final_g)
    stk = lambda sts, j: jnp.stack([st[j] for st in sts], axis=0)
    return (y_prompt, y_sample,
            stk(p_states, 0), stk(p_states, 1), stk(p_states, 2), stk(p_states, 3), stk(p_states, 4), stk(p_states, 5),
            stk(s_states, 0), stk(s_states, 1), stk(s_states, 2), stk(s_states, 3), stk(s_states, 4), stk(s_states, 5))


_drawn_inputs = setup_inputs


def setup_inputs(seed=0):
    import zlib

    import numpy as np

    out = dict(_drawn_inputs(seed))
    spreads = {}
    factors = {'norm2_g': 6.606,
     'lru_ba': 8.0,
     'lru_bx': 8.0,
     'mlstm_norm_g': 8.0,
     'pool_scale': 8.0,
     'final_g': 2.723}
    for name, (base, spread) in spreads.items():
        noise = np.random.default_rng([zlib.crc32(name.encode()), seed]).standard_normal(out[name].shape)
        drawn = base * np.exp(spread * noise) if base else spread * noise
        out[name] = __import__('jax').numpy.asarray(drawn.astype(out[name].dtype))
    for name, factor in factors.items():
        out[name] = (out[name] * factor).astype(out[name].dtype)
    return out
```

```python
from contextlib import ExitStack

import numpy as np

import concourse.bass as bass
from concourse import mybir

ALU = mybir.AluOpType
ACT = mybir.ActivationFunctionType
AX_X = mybir.AxisListType.X
F32 = mybir.dt.float32
F32R = mybir.dt.float32r

P = 128
D = 1024
SEQ = 1024
DEC = 8
TOK = SEQ + DEC
CH = TOK // 3
NCH = 3
LAST = CH - DEC
KT = D // P
LRU_T = 3
ML_T = 3
POOL_T = 2
HEADS, HD = 4, 96
HV = HD + 1
CONV = 4
WINS = (2, 4, 8, 16)
PBUF = 15
EPS = 1e-6
LC = 128
NLC = SEQ // LC
ROWS = HEADS * (NLC + 1)
VCOLS = HEADS * HD + 2 * HEADS
FF_BLOCKS = 4
NADA = 6 * KT
ADA_FIRST = 2 * KT
N_MIX = 2 * LRU_T + 3 * ML_T + POOL_T
N_KQO = LRU_T + 3 * ML_T
N_OUT = KT
N_FF = FF_BLOCKS * 2 * KT
N_UNITS = N_MIX + N_OUT + N_FF
RAW = 4
FUS = 4
NEG_BIG = -3.0e38

_COLS = {}
_at = 0
for _n, _w in (("g1", KT), ("g2", KT), ("gf", KT), ("b_ada", NADA), ("conv_w", LRU_T * CONV), ("conv_b", LRU_T),
               ("ba", LRU_T), ("bx", LRU_T), ("lam", LRU_T), ("pool_scale", POOL_T), ("inv_win", POOL_T),
               ("ml_g", ML_T), ("fix", POOL_T * PBUF), ("h0", LRU_T * DEC)):
    _COLS[_n] = (_at, _at + _w)
    _at += _w
NCOLS = _at


def plan_mix():
    p = [("NORM", c) for c in range(NCH)]
    p += [("V", t) for t in range(NLC + 1)]
    ada = [("ADA", j) for j in range(ADA_FIRST, NADA)]

    def unit(u, between=((), (), ())):
        for c in range(NCH):
            p.append(("D", u, c))
            p.extend(between[c])
        for _ in range(2):
            if ada:
                p.append(ada.pop(0))

    unit(0, ([("G1",)], [("G2",)], [("LRUC", 0)]))
    unit(1, ([("G3",)], [("LRUG", 0)], [("G4",), ("LRUC", 1)]))
    unit(2, ([("LRUG", 1)], [], [("LRUC", 2)]))
    unit(3, ([("LRUG", 2)], [], []))
    unit(4), unit(5)
    unit(6), unit(7), unit(8, ([], [], [("TS",), ("LD", 0), ("SMA",)]))
    for i in range(8):
        y = {3: [0, 1], 4: [2, 3], 5: [4], 6: [5], 7: [6]}.get(i, [])
        p.append(("S", i))
        if i + 1 < NLC:
            p.append(("LD", i + 1))
        tail = [("U", i)]
        extra = {1: [("SMB",)], 2: [("SMC",)], 3: [("YS",)], 4: [("POOL", 0)], 5: [("POOL", 1)]}.get(i, [])
        unit(9 + i, ([("AB", i)], tail, [("Y", c) for c in y] + extra))
    p.append(("Y", 7))
    while ada:
        p.append(ada.pop(0))
    return p


UNIT_KIND = [("xr", t) for t in range(3)] + [("k", t) for t in range(3)] + [("q", t) for t in range(3)] + \
            [("o", t) for t in range(3)] + [("u", t) for t in range(2)] + [("gr", t) for t in range(3)]
AUX = ["X0", "X1", "X2", "X3", "X4"]


def bank_uses(plan):
    count = {b: 0 for b in AUX}
    use = {}

    def add(key, bank):
        use[key] = (bank, count[bank])
        count[bank] += 1

    for j in range(ADA_FIRST):
        add(("ADA", j), "X4")
    for s in plan:
        k = s[0]
        if k == "NORM":
            add(s, "X0")
        elif k == "V":
            add(s, ("X1", "X2")[s[1] % 2])
        elif k == "ADA":
            add(s, "X4")
        elif k in ("G1", "G2", "G3", "G4", "Y", "YS"):
            add(s, "X3")
        elif k == "TS":
            for w in range(2):
                add(("TS", w), "X3")
        elif k == "LRUG":
            for g in range(2):
                for c in range(NCH):
                    add((*s, g, c), ("X0", "X1", "X2")[c])
        elif k == "S":
            add(("S", s[1]), "X0")
            add(("KT", s[1]), "X3")
        elif k == "AB":
            add(("A", s[1]), "X1")
            add(("B", s[1]), "X2")
        elif k == "U":
            add(s, "X0")
        elif k == "POOL":
            for c in range(NCH):
                add((*s, c), ("X1", "X2")[c % 2])
    for n in (2, 3):
        for c in range(NCH):
            add(("NORM", n, c), "X0")
    return use


class Rise:

    def __init__(self, sem):
        self.sem, self.base, self.off = sem, 0, 0

    @property
    def at(self):
        return self.base + self.off

    def enter(self, i, per):
        self.before, self.per = self.at, per
        self.base, self.off = self.before + i * per, 0

    def leave(self, times):
        assert self.off == self.per, (self.off, self.per)
        self.base, self.off = self.before + times * self.per, 0



def plan_pieces(plan):
    out = []
    for s in plan:
        if s[0] == "NORM":
            out += [(("N", s[1], kt), ("H", kt, s[1] * CH, CH)) for kt in range(KT)]
        elif s[0] == "D" and UNIT_KIND[s[1]][0] == "gr":
            out.append((s, ("Y", UNIT_KIND[s[1]][1], s[2] * CH, CH)))
        elif s[0] == "Y":
            out.append((s, ("Y3", LRU_T, s[1] * LC, LC)))
        elif s[0] == "YS":
            out.append((s, ("Y3", LRU_T, SEQ, DEC)))
        elif s[0] == "POOL":
            out += [((*s, c), ("Y", LRU_T + ML_T + s[1], c * CH, CH)) for c in range(NCH)]
    return out


def build(nc, I, O):
    plan = plan_mix()
    use = bank_uses(plan)
    pieces = plan_pieces(plan)
    full_at = {k: n for n, (k, _) in enumerate(pieces)}
    target = dict(pieces)
    P_MIX = len(pieces)
    P_FF = P_MIX + NCH * KT
    assert P_MIX % FUS == 0
    raw_seq = [("ADA", j) for j in range(ADA_FIRST)]
    for s in plan:
        if s[0] == "D" and s[2] == 0:
            raw_seq.append(("W", s[1]))
        elif s[0] == "ADA":
            raw_seq.append(s)
    assert len(raw_seq) == N_MIX + NADA
    raw_seq += [("W", u) for u in range(N_MIX, N_MIX + RAW)]
    raw_at = {k: n for n, k in enumerate(raw_seq)}

    PER = NCH * RAW
    SQ_OUT, SQ_LAST = NCH * KT, 2 * NCH * KT
    U_FF = N_MIX + N_OUT
    U_LAST = U_FF + (FF_BLOCKS - 1) * 2 * KT
    P_LAST = P_FF + (FF_BLOCKS - 1) * NCH * KT
    N_LD_S = 4 * (DEC + 2) + DEC + 3
    with ExitStack() as ctx:
        SLOT = TOK * 4
        top = [nc.sbuf_base + (-nc.sbuf_base) % 32]

        def region(size):
            a = top[0]
            top[0] += size + (-size) % 32
            return a

        def at(name, shape, off, dt=F32):
            return nc.alloc_sbuf_tensor_at(name, shape, dt, offset=off)

        def new(name, shape, dt=F32):
            return at(name, shape, region(int(np.prod(shape[1:])) * 4), dt)

        rH = top[0]
        H_hi = new("H_hi", [P, KT, TOK], F32R)
        H_lo = new("H_lo", [P, KT, TOK], F32R)
        rY = region(2 * KT * SLOT)
        Y_hi = at("Y_hi", [P, KT, TOK], rY, F32R)
        Y_lo = at("Y_lo", [P, KT, TOK], rY + KT * SLOT, F32R)
        RAWW = new("RAWW", [P, RAW, KT * P])
        W_hi = new("W_hi", [P, 2, KT * P], F32R)
        W_lo = new("W_lo", [P, 2, KT * P], F32R)
        rX = region(KT * SLOT)
        X = at("X", [P, KT, TOK], rX)

        slot = [rY + k * SLOT for k in range(2 * KT)]
        X0T = at("X0T", [P, KT, TOK], rY)
        WV_hi = at("WV_hi", [P, KT, VCOLS], slot[8], F32R)
        XR = [at(f"XR{t}", [P, SEQ + CONV - 1], slot[3 + t]) for t in range(3)]
        XC, RG = at("XC", [P, TOK], slot[6]), at("RG", [P, TOK], slot[7])
        IG, AG, TH = at("IG", [P, TOK], slot[11]), at("AG", [P, TOK], slot[12]), at("TH", [P, TOK], slot[13])
        BT, MU = at("BT", [P, TOK], slot[14]), at("MU", [P, TOK], slot[15])
        HS = [at(f"HS{t}", [P, TOK], slot[8 + t]) for t in range(3)]
        PA = [at(f"PA{j}", [P, TOK], slot[14 + j]) for j in range(2)]
        PB = [at(f"PB{j}", [P, TOK], slot[6 + j]) for j in range(2)]
        OUTN = at("OUTN", [P, KT, TOK], rY)

        WV_raw = at("WV_raw", [P, KT, VCOLS], rX)
        WV_lo = at("WV_lo", [P, KT, VCOLS], rX + KT * VCOLS * 4, F32R)
        VS = [at(f"VS{b}", [P, HEADS, HV], rX + 2 * KT * VCOLS * 4 + 1568 * b) for b in range(2)]
        inx_at = [rX]

        def inx(name, shape):
            a, size = inx_at[0], int(np.prod(shape[1:])) * 4
            inx_at[0] += size + (-size) % 32
            assert inx_at[0] <= rX + KT * SLOT, name
            return at(name, shape, a)

        K96 = [inx(f"K96_{b}", [HD, HEADS, LC]) for b in range(2)]
        Q96 = [inx(f"Q96_{b}", [HD, HEADS, LC]) for b in range(2)]
        VB = [inx(f"VB{b}", [P, HEADS, HV]) for b in range(2)]
        NM, EX = inx("NM", [P, HEADS, LC]), inx("EX", [P, HEADS, LC])
        KW, CN = inx("KW", [P, HEADS, HD]), inx("CN", [HD, HEADS, HV])
        T1, NUM = inx("T1", [P, HEADS, HV]), inx("NUM", [P, HEADS, HV])
        HM = [inx(f"HM{b}", [P, HEADS, HD]) for b in range(4)]
        OT = inx("OT", [P, ML_T, LC])

        FU = new("FU", [P, FUS, 3 * LC])
        ST = [new(f"ST{b}", [P, TOK]) for b in range(2)]
        rN = region(2 * CH * 4 + SLOT + CH * 4)
        SQ, SS, RS = at("SQ", [P, 2, CH], rN), at("SS", [P, TOK], rN + 2 * CH * 4), at("RS", [P, CH], rN + 2 * CH * 4 + SLOT)
        GT = at("GT", [P, 2, CH], rN)
        MOD, CTX = new("MOD", [P, NADA, DEC + 1]), new("CTX", [P, KT, DEC + 1])
        CTS = at("CTS", [P, KT, DEC + 1], rH)
        COLS, IDN, ONE = new("COLS", [P, NCOLS]), new("IDN", [P, P]), new("ONE", [P, P])
        EPT, LS = new("EPT", [P, 1]), new("LS", [P, 6, LRU_T])
        XS, OUTC = new("XS", [P, LRU_T, DEC, CONV]), new("OUTC", [P, LRU_T, CONV - 1])
        OUTL = new("OUTL", [P, LRU_T, DEC + 1])
        SG = inx("SG", [P, 3 * ML_T, DEC])
        BDL = at("BDL", [P, 2 * LRU_T, P], slot[0])
        BDP = new("BDP", [P, POOL_T, P])
        UB, UO, UM = new("UB", [P, POOL_T, DEC, PBUF + 1]), new("UO", [P, POOL_T, PBUF]), new("UM", [P, DEC])
        MASK, T8 = inx("MASK", [P, LC]), new("T8", [P, DEC])
        GTE = inx("GTE", [P, 2 * HEADS, NLC + 1])
        VS8 = inx("VS8", [DEC, HEADS * HD])
        QK8 = at("QK8", [DEC, 2, HEADS * HD], slot[14])
        HS8 = at("HS8", [DEC, HEADS * HD], slot[14] + 2 * HEADS * HD * 4)
        GR = at("GR", [ROWS, 14, LC], rN)
        R_I, R_F, R_T, R_U, R_LN, R_C, R_LF, R_BC, R_A, R_INT, R_M, R_NM, R_W, R_EM = range(14)
        GB, M0, SR = new("GB", [ROWS, 2]), new("M0", [ROWS, DEC]), new("SR", [ROWS, DEC, 4])
        MPC, BM, MP = new("MPC", [ROWS, 1]), new("BM", [1, 2 * ROWS]), new("MP", [1, ROWS])
        COL, DECB = inx("COL", [P, 4, ROWS]), inx("DECB", [HD, ROWS])
        SM4 = new("SM4", [P, 8, HEADS])
        VH = HD // 4
        CS, TC = at("CS", [P, VH, HD], slot[11]), at("TC", [P, VH // 4, HD], slot[11] + VH * HD * 4)
        small = [slot[14] + 3 * HEADS * HD * 4 + i * HD * 4 for i in range(8)]
        K128, Q128 = at("K128", [P, HD], small[0]), at("Q128", [P, HD], small[1])
        V24, H24, S128 = at("V24", [P, VH], small[7]), at("H24", [P, VH], small[7] + 96), at("S128", [P, 4], small[7] + 192)
        K32, Q32, N32, H32, T32 = (at(n, [DEC * HEADS, HD], small[2 + i]) for i, n in enumerate(("K32", "Q32", "N32", "H32", "T32")))
        S32, D32 = at("S32", [DEC * HEADS, 4], small[7] + 224), at("D32", [DEC * HEADS, 8], small[7] + 256)
        assert top[0] <= nc.sbuf_usable_end, (top[0], nc.sbuf_usable_end)

        DB = [ctx.enter_context(nc.psum_tensor(f"D{c}", [P, 512], F32)) for c in range(NCH)]
        XB = {n: ctx.enter_context(nc.psum_tensor(n, [P, 512], F32)) for n in AUX}

        def dram(name, shape):
            return nc.dram_tensor(name, shape, F32).ap()

        k_d, q_d, o_d = (dram(n, [ML_T * P, SEQ]) for n in ("k_d", "q_d", "o_d"))
        v_d = dram("v_d", [NLC, P, HEADS * HV])
        sv_d, sk_d, sq_d, sh_d, sy_d = (dram(n, [DEC, HEADS * HD]) for n in ("sv_d", "sk_d", "sq_d", "sh_d", "sy_d"))
        nm_d, dec_d, sr_d = dram("nm_d", [ROWS, LC]), dram("dec_d", [ROWS, 1]), dram("sr_d", [ROWS, DEC, 4])

        def col(name, k=0, n=1, p0=0, p1=P):
            a = _COLS[name][0] + k
            return COLS[p0:p1, a:a + n]

        def heads(ap):
            return ap.rearrange("p (h d) -> p h d", h=HEADS)

        def colh(k, c):
            return COL[:, k, :].rearrange("p (h c) -> p h c", c=NLC + 1)[:, :, c]

        def wide(ap, n):
            return ap.unsqueeze(2).to_broadcast([ap.shape[0], ap.shape[1], n])

        def over(ap, n):
            return ap.unsqueeze(1).to_broadcast([ap.shape[0], n, ap.shape[1]])

        def tile(t, i, a, b):
            if isinstance(i, int):
                return t[:, i, a:b]
            return t[:, bass.ds(i, 1), a:b].rearrange("p a n -> p (a n)")

        def sem(name):
            return ctx.enter_context(nc.semaphore(name))

        d_full = [sem(f"dense{c}_full") for c in range(NCH)]
        d_free = [sem(f"dense{c}_free") for c in range(NCH)]
        x_full = {b: sem(f"{b}_full") for b in AUX}
        x_free = {b: sem(f"{b}_free") for b in AUX}
        raw_in = [sem(f"raw{r}_in") for r in range(RAW)]
        w_hi_ready, w_lo_ready = sem("w_hi_ready"), sem("w_lo_ready")
        full_ready = sem("full_ready")
        hi_ready, lo_ready = sem("hi_ready"), sem("lo_ready")
        sq_ready, ss_done = sem("sq_ready"), sem("ss_done")
        ss_zero = sem("ss_zero")
        act_step, dve_step = sem("act_step"), sem("dve_step")
        ld_x = [sem(f"ld_x{c}") for c in range(NCH)]
        ld_small, ld_c, ld_wv, ld_xres = sem("ld_small"), sem("ld_c"), sem("ld_wv"), sem("ld_xres")
        ones_ready, sig_c, c_ready = sem("ones_ready"), sem("sig_c"), sem("c_ready")
        sd_ready, rs_ready = sem("sd_ready"), sem("rs_ready")
        wv_hi, wv_lo = sem("wv_hi"), sem("wv_lo")
        v_ready, v8_ready, v8_stored = sem("v_ready"), sem("v8_ready"), sem("v8_stored")
        v_stored = [sem(f"v_stored{b}") for b in range(2)]
        st_stored = [sem(f"st_stored{b}") for b in range(2)]
        ga, gv = sem("gate_rows_act"), sem("gate_rows_dve")
        nm_ready, nm_stored, int_ready, dec_stored, ld_dec = (sem(n) for n in (
            "nm_ready", "nm_stored", "int_ready", "dec_stored", "ld_dec"))
        la, lv = sem("lam_act"), sem("lam_dve")
        xc_ready, ah_ready, m2_ready, mult_ready, h_ready = (sem(n) for n in (
            "xc_ready", "ah_ready", "m2_ready", "mult_ready", "h_ready"))
        ts_stored, u_diff = sem("ts_stored"), sem("u_diff")
        ld_kqv = [sem(f"ld_kqv{b}") for b in range(2)]
        ld_nm, ld_o = sem("ld_nm"), sem("ld_o")
        ex_ready, ex_exp, s_ready, cn_ready = sem("ex_ready"), sem("ex_exp"), sem("s_ready"), sem("cn_ready")
        z_ready, z_root, hm_ready = sem("z_ready"), sem("z_root"), sem("hm_ready")
        sma_t, sma_e, sr_stored = sem("sma_t"), sem("sma_e"), sem("sr_stored")
        ld_st, ld_s, ld_bdl = sem("ld_state"), sem("ld_s"), sem("ld_bdl")
        smb_h, h_stored, ld_h32 = sem("smb_h"), sem("h_stored"), sem("ld_h32")
        smc_z, smc_root, smc_y, y_stored, ld_y8 = (sem(n) for n in ("smc_z", "smc_root", "smc_y", "y_stored", "ld_y8"))
        x_upd, relu_ready = sem("x_upd"), sem("relu_ready")
        fin_ready, out_done = sem("fin_ready"), sem("out_done")
        c_out, s_out = sem("c_out"), sem("s_out")

        def st_count(u, b):
            return sum(v % 2 == b for v in range(LRU_T, u))

        def raw_wait(e, key):
            n = raw_at[key]
            e.wait_ge(raw_in[n % RAW], 16 * (n // RAW + 1))
            return n % RAW

        def raw_slot(u):
            return raw_at[("W", u)] % RAW

        def bank(key):
            return XB[use[key][0]]

        def wait_full(e, key):
            b, n = use[key]
            e.wait_ge(x_full[b], n + 1)

        def free(key):
            return x_free[use[key][0]]

        block = ctx.enter_context(nc.Block())

        @block.sync
        def _(sp):
            for dst, name in ((COLS, "cols"), (IDN, "ident"), (BDP, "bdp"), (XS, "conv_state"),
                              (UB, "pool_buf"), (MASK, "mask"), (GB, "gate_bias"), (M0, "m0")):
                sp.dma_start(dst[:], I[name]).then_inc(ld_small, 16)
            sp.dma_start(CTX[:], I["c"]).then_inc(ld_c, 16)
            x_v = I["x"].rearrange("(k p) t -> p k t", p=P)
            for c in range(NCH):
                sp.dma_start(X0T[:, :, c * CH:(c + 1) * CH], x_v[:, :, c * CH:(c + 1) * CH]).then_inc(ld_x[c], 16)
            nload = [0]

            def occupant_done(n):
                kind, j = raw_seq[n - RAW]
                if kind == "ADA":
                    wait_full(sp, ("ADA", j))
                else:
                    sp.wait_ge(w_lo_ready, j + 1)

            def load_raw():
                n = nload[0]
                if n < len(raw_seq):
                    nload[0] += 1
                    if n >= RAW:
                        occupant_done(n)
                    kind, j = raw_seq[n]
                    sp.dma_start(RAWW[:, n % RAW, :], I["WADA" if kind == "ADA" else "W"][j]).then_inc(raw_in[n % RAW], 16)

            for _ in range(RAW):
                load_raw()
            sp.dma_start(WV_raw[:], I["wv"]).then_inc(ld_wv, 16)
            for _ in range(ADA_FIRST):
                load_raw()
            sp.wait_ge(full_ready, NCH * KT)
            sp.dma_start(BDL[:], I["bdl"]).then_inc(ld_bdl, 16)
            for s in plan:
                k = s[0]
                if k == "V":
                    t = s[1]
                    if t < NLC:
                        sp.wait_ge(v_ready, t + 1)
                        sp.dma_start(v_d[t], VS[t % 2][:].rearrange("p h v -> p (h v)")).then_inc(v_stored[t % 2], 16)
                    else:
                        sp.wait_ge(v8_ready, 1)
                        sp.dma_start(sv_d, VS8[:]).then_inc(v8_stored, 16)
                elif k == "G3":
                    sp.wait_ge(nm_ready, 1)
                    sp.dma_start(nm_d, GR[:, R_NM, :]).then_inc(nm_stored, 16)
                    sp.wait_ge(int_ready, 1)
                    sp.dma_start(dec_d, GR[:, R_INT, LC - 1:LC]).then_inc(dec_stored, 16)
                    sp.wait_ge(dec_stored, 16)
                    sp.dma_start(DECB[:], dec_d.rearrange("r a -> (r a)").partition_broadcast(HD)).then_inc(ld_dec, 16)
                elif k == "ADA":
                    load_raw()
                elif k == "D" and s[2] == NCH - 1:
                    u = s[1]
                    load_raw()
                    kind, t = UNIT_KIND[u]
                    if kind in ("k", "q", "o"):
                        for c in range(NCH):
                            sp.wait_ge(d_free[c], u + 1)
                        dst = {"k": k_d, "q": q_d, "o": o_d}[kind]
                        sp.dma_start(dst[t * P:(t + 1) * P, :], ST[u % 2][:, 0:SEQ]).then_inc(st_stored[u % 2], 16)
                elif k == "TS":
                    sp.wait_ge(h_ready, LRU_T)
                    sp.dma_start(CS[:], I["C"]).then_inc(ld_st, 16)
                    sp.dma_start(N32[:], I["n"]).then_inc(ld_st, 16)
                    sp.wait_ge(x_free["X3"], use[("TS", 1)][1] + 1)
                    sp.dma_start(sk_d, QK8[:, 0, :]).then_inc(ts_stored, 16)
                    sp.dma_start(sq_d, QK8[:, 1, :]).then_inc(ts_stored, 16)
                elif k == "LD":
                    c = s[1]
                    b = c % 2
                    if c == 0:
                        for i in range(2):
                            sp.wait_ge(st_stored[i], 16 * ML_T)
                            sp.wait_ge(v_stored[i], 16 * NLC // 2)
                        sp.wait_ge(nm_stored, 16)
                        sp.wait_ge(v8_ready, 1)
                    if c >= 2:
                        wait_full(sp, ("U", c - 2))
                        wait_full(sp, ("B", c - 2))
                    for src, dst in ((k_d, K96[b]), (q_d, Q96[b])):
                        sp.dma_start(dst[:], src.rearrange("(h d) t -> d h t", d=HD)[:, :, c * LC:(c + 1) * LC]).then_inc(ld_kqv[b], 16)
                    sp.dma_start(VB[b][:].rearrange("p h v -> p (h v)"), v_d[c]).then_inc(ld_kqv[b], 16)
                    if c >= 1:
                        sp.wait_ge(ex_ready, c)
                    sp.dma_start(NM[:], nm_d.rearrange("(h c) t -> c h t", c=NLC + 1)[c].partition_broadcast(P)).then_inc(ld_nm, 16)
                elif k == "SMA":
                    sp.wait_ge(sma_e, 2)
                    sp.dma_start(sr_d, SR[:]).then_inc(sr_stored, 16)
                    sp.dma_start(O["m_s"], SR[:]).then_inc(out_done, 16)
                    sp.wait_ge(sr_stored, 16)
                    sp.wait_ge(ts_stored, 32)
                    sp.wait_ge(v8_stored, 16)
                    rows = sr_d.rearrange("(h c) b k -> c b h k", c=NLC + 1)[NLC]
                    for q in range(4):
                        for b_ in range(DEC):
                            p0 = b_ * 16 + q
                            sp.dma_start(S128[p0:p0 + 13:4, :], rows[b_]).then_inc(ld_s, 16)
                        sp.dma_start(K128[q::4, :], sk_d.rearrange("b (h d) -> (b h) d", d=HD)).then_inc(ld_s, 16)
                        sp.dma_start(Q128[q::4, :], sq_d.rearrange("b (h d) -> (b h) d", d=HD)).then_inc(ld_s, 16)
                    for b_ in range(DEC):
                        sp.dma_start(S32[b_ * 4:b_ * 4 + 4, :], rows[b_]).then_inc(ld_s, 16)
                    sp.dma_start(K32[:], sk_d.rearrange("b (h d) -> (b h) d", d=HD)).then_inc(ld_s, 16)
                    sp.dma_start(Q32[:], sq_d.rearrange("b (h d) -> (b h) d", d=HD)).then_inc(ld_s, 16)
                    sp.dma_start(V24[:], sv_d.rearrange("b (x v) -> (b x) v", v=VH)).then_inc(ld_s, 16)
                elif k == "SMB":
                    sp.wait_ge(smb_h, 1)
                    sp.dma_start(sh_d.rearrange("b (x v) -> (b x) v", v=VH), H24[:]).then_inc(h_stored, 16)
                    sp.wait_ge(h_stored, 16)
                    sp.dma_start(H32[:], sh_d.rearrange("b (h d) -> (b h) d", d=HD)).then_inc(ld_h32, 16)
                    sp.dma_start(O["C_s"], CS[:]).then_inc(s_out, 16)
                    sp.dma_start(O["n_s"], N32[:]).then_inc(s_out, 16)
                elif k == "SMC":
                    sp.wait_ge(smc_y, 1)
                    sp.dma_start(sy_d.rearrange("b (h d) -> (b h) d", d=HD), H32[:]).then_inc(y_stored, 16)
                    sp.wait_ge(y_stored, 16)
                    sp.dma_start(HS8[:], sy_d).then_inc(ld_y8, 16)
                elif k == "Y":
                    c = s[1]
                    if c == 0:
                        for i in range(2):
                            sp.wait_ge(st_stored[i], 16 * st_count(N_KQO, i))
                    else:
                        sp.wait_ge(full_ready, full_at[("Y", c - 1)] + 1)
                    sp.dma_start(OT[:], o_d.rearrange("(j p) t -> p j t", p=P)[:, :, c * LC:(c + 1) * LC]).then_inc(ld_o, 16)
            assert nload[0] == len(raw_seq), nload
            b, n = use[("U", NLC - 1)]
            sp.wait_ge(x_free[b], n + 1)
            sp.dma_start(O["C_p"], CN[:]).then_inc(c_out, 16)
            sp.wait_ge(full_ready, full_at[("Y", NLC - 1)] + 1)
            sp.wait_ge(c_out, 16)
            for m in range(KT):
                sp.dma_start(X[:, m, :], I["x"][m * P:(m + 1) * P, :]).then_inc(ld_xres, 16)
            sp.dma_start(O["m_p"], MP[:]).then_inc(out_done, 16)
            sp.wait_ge(h_ready, LRU_T)
            sp.dma_start(O["lru"], OUTL[:]).then_inc(out_done, 16)
            sp.dma_start(O["conv_p"], OUTC[:]).then_inc(out_done, 16)
            sp.dma_start(O["conv_s"], XS[:]).then_inc(out_done, 16)
            sp.wait_ge(u_diff, POOL_T)
            sp.dma_start(O["pool_p"], UO[:]).then_inc(out_done, 16)
            sp.dma_start(O["pool_s"], UB[:]).then_inc(out_done, 16)
            with sp.Fori(0, (N_OUT + N_FF - RAW) // RAW) as g:
                for j in range(RAW):
                    r = (N_MIX + NADA + j) % RAW
                    sp.wait_ge(w_lo_ready, g * RAW + (N_MIX + j + 1))
                    sp.dma_start(RAWW[:, r, :], I["W"][bass.ds(g * RAW + (N_MIX + RAW + j), 1)].rearrange("a p n -> p (a n)")
                                 ).then_inc(raw_in[r], 16)
            sp.wait_ge(w_lo_ready, N_UNITS - RAW + 1)
            sp.dma_start(RAWW[:, (N_UNITS + NADA) % RAW, :], I["W"][N_UNITS - 1]).then_inc(raw_in[(N_UNITS + NADA) % RAW], 16)
            y_v = O["y"].rearrange("(k p) t -> p k t", p=P)
            for c in range(NCH):
                for kt in range(KT):
                    sp.wait_ge(fin_ready, c * KT + kt + 1)
                    sp.dma_start(y_v[:, kt, c * CH:(c + 1) * CH], OUTN[:, kt, c * CH:(c + 1) * CH]).then_inc(out_done, 16)
            sp.wait_ge(s_out, 32)
            sp.wait_ge(out_done, 16 * (7 + NCH * KT))

        def views(key):
            kind, kt, t0, n = target[key]
            hi, lo = (H_hi, H_lo) if kind == "H" else (Y_hi, Y_lo)
            f = full_at[key] % FUS
            if kind == "Y3":
                return hi[:, kt:kt + 3, t0:t0 + n], lo[:, kt:kt + 3, t0:t0 + n], \
                    FU[:, f, 0:3 * n].rearrange("p (j t) -> p j t", j=3)
            return hi[:, kt, t0:t0 + n], lo[:, kt, t0:t0 + n], FU[:, f, 0:n]

        def norm2_views(n):
            c, kt = n // KT, n % KT
            a, b = c * CH, (c + 1) * CH
            return H_hi[:, kt, a:b], H_lo[:, kt, a:b], FU[:, (P_MIX + n) % FUS, 0:CH]

        @block.gpsimd
        def _(pool):
            def w_lo(u, raw, s):
                pool.wait_ge(w_hi_ready, u + 1)
                nc.gpsimd.tensor_tensor(W_lo[:, s, :], RAWW[:, raw, :], W_hi[:, s, :].bitcast(F32),
                                        ALU.subtract).then_inc(w_lo_ready, 1)

            def lo(n, hi_v, lo_v, fu_v):
                pool.wait_ge(hi_ready, n + 1)
                nc.gpsimd.tensor_tensor(lo_v, fu_v, hi_v.bitcast(F32), ALU.subtract).then_inc(lo_ready, 1)

            def add_square(n, c, s):
                pool.wait_ge(sq_ready, n + 1)
                nc.gpsimd.tensor_tensor(SS[:, c * CH:(c + 1) * CH], SS[:, c * CH:(c + 1) * CH], SQ[:, s, :],
                                        ALU.add).then_inc(ss_done, 1)
                pool.wait_ge(ss_done, n + 1)

            nc.gpsimd.memset(SS[:], 0.0).then_inc(ss_zero, 1)
            pool.wait_ge(ss_zero, 1)
            for n in range(NCH * KT):
                add_square(n, n // KT, n % 2)
            pool.wait_ge(wv_hi, 1)
            nc.gpsimd.tensor_tensor(WV_lo[:], WV_raw[:], WV_hi[:].bitcast(F32), ALU.subtract).then_inc(wv_lo, 1)
            w_lo(0, raw_slot(0), 0)
            for s in plan:
                k = s[0]
                if k == "NORM":
                    for kt in range(KT):
                        lo(full_at[("N", s[1], kt)], *views(("N", s[1], kt)))
                elif k == "D":
                    if s[2] == 0:
                        w_lo(s[1] + 1, raw_slot(s[1] + 1), (s[1] + 1) % 2)
                    if s in full_at:
                        lo(full_at[s], *views(s))
                elif k in ("Y", "YS"):
                    if k == "Y" and s[1] == 0:
                        pool.wait_ge(s_out, 32)
                    lo(full_at[s], *views(s))
                elif k == "POOL":
                    for c in range(NCH):
                        lo(full_at[(*s, c)], *views((*s, c)))

            def clear(norm):
                wait_full(pool, norm)
                nc.gpsimd.memset(SS[:], 0.0).then_inc(ss_zero, 1)

            def units(first, g, hidden=None, piece=None, square=None):
                for j in range(RAW):
                    w_lo(g * RAW + (first + j + 1), (first + j + 1 + NADA) % RAW, (first + j + 1) % 2)
                    for c in range(NCH):
                        q = NCH * j + c
                        if hidden is not None:
                            f = hidden * RAW + j
                            lo(piece + q, tile(Y_hi, f, c * CH, (c + 1) * CH),
                               tile(Y_lo, f, c * CH, (c + 1) * CH), FU[:, q % FUS, 0:CH])
                        if square is not None:
                            add_square(square + q, c, q % 2)

            clear(("NORM", NCH - 1))
            pool.wait_ge(ss_zero, 2)
            with pool.Fori(0, N_OUT // RAW) as g:
                units(N_MIX, g, square=g * PER + SQ_OUT)
            for n in range(NCH * KT):
                lo(P_MIX + n, *norm2_views(n))
            clear(("NORM", 2, NCH - 1))
            pool.wait_ge(ss_zero, 3)
            with pool.Fori(0, FF_BLOCKS - 1) as b:
                with pool.Fori(0, KT // RAW) as g:
                    units(U_FF, b * 4 + g, hidden=g, piece=b * (2 * PER) + g * PER + P_FF)
                with pool.Fori(0, KT // RAW) as g:
                    units(U_FF + KT, b * 4 + g)
            with pool.Fori(0, KT // RAW) as g:
                units(U_LAST, g, hidden=g, piece=g * PER + P_LAST)
            with pool.Fori(0, KT // RAW) as g:
                units(U_LAST + KT, g, square=g * PER + SQ_LAST)

        @block.scalar
        def _(act):
            step = Rise(act_step)

            def link(ins):
                step.off += 1
                ins.then_inc(act_step, 1)
                act.wait_ge(act_step, step.at)

            def w_hi(u, raw, s, landed):
                act.wait_ge(raw_in[raw], landed)
                if not (isinstance(u, int) and u < 2):
                    act.wait_ge(d_full[NCH - 1], u - 1)
                nc.scalar.activation(W_hi[:, s, :], RAWW[:, raw, :], ACT.Copy).then_inc(w_hi_ready, 1)

            def hi(n, hi_v, fu_v):
                act.wait_ge(full_ready, n + 1)
                nc.scalar.activation(hi_v, fu_v, ACT.Copy).then_inc(hi_ready, 1)

            def hi_key(key):
                h, _, f = views(key)
                hi(full_at[key], h, f)

            def root(norm, read):
                wait_full(act, norm)
                if read:
                    act.wait_ge(full_ready, read)
                nc.scalar.activation(RS[:], bank(norm)[:, 0:CH], ACT.Sqrt, bias=EPT[:], scale=1.0 / D).then_inc(free(norm), 1)

            act.wait_ge(ld_c, 16)
            nc.scalar.activation(CTS[:], CTX[:], ACT.Sigmoid).then_inc(sig_c, 1)
            act.wait_ge(ld_small, 16 * 8)
            link(nc.scalar.activation(LS[:, 0, :], col("lam", 0, LRU_T), ACT.Abs))
            nc.scalar.activation(LS[:, 0, :], LS[:, 0, :], ACT.Exp, scale=-1.0).then_inc(la, 1)
            act.wait_ge(lv, 1)
            nc.scalar.activation(LS[:, 2, :], LS[:, 1, :], ACT.Ln).then_inc(la, 1)
            for n in range(NCH * KT):
                c, kt = n // KT, n % KT
                act.wait_ge(ld_x[c], 16)
                if n >= 2:
                    act.wait_ge(ss_done, n - 1)
                nc.scalar.activation(SQ[:, n % 2, :], X0T[:, kt, c * CH:(c + 1) * CH], ACT.Square).then_inc(sq_ready, 1)
            act.wait_ge(ld_wv, 16)
            nc.scalar.activation(WV_hi[:], WV_raw[:], ACT.Copy).then_inc(wv_hi, 1)
            w_hi(0, raw_slot(0), 0, 16 * (raw_at[("W", 0)] // RAW + 1))
            act.wait_ge(ones_ready, 6)
            for s in plan:
                k = s[0]
                if k == "NORM":
                    c = s[1]
                    root(s, c * KT)
                    for kt in range(KT):
                        hi_key(("N", c, kt))
                elif k == "D":
                    _, u, c = s
                    a, b = c * CH, (c + 1) * CH
                    if c == 0:
                        v = u + 1
                        seq = raw_at[("W", v)]
                        w_hi(v, seq % RAW, v % 2, 16 * (seq // RAW + 1))
                    act.wait_ge(d_full[c], u + 1)
                    kind, t = UNIT_KIND[u]
                    src = DB[c][:, 0:CH]
                    samples = DB[c][:, LAST:CH]
                    if kind == "xr":
                        n = CH if c < NCH - 1 else LAST
                        if c == NCH - 1:
                            link(nc.scalar.activation(XS[:, t, :, CONV - 1], samples, ACT.Copy))
                        nc.scalar.activation(XR[t][:, CONV - 1 + a:CONV - 1 + a + n], DB[c][:, 0:n], ACT.Copy).then_inc(d_free[c], 1)
                    elif kind in ("k", "q", "o"):
                        n = u - 3
                        fn, scale = (ACT.Sigmoid, 1.0) if kind == "o" else (ACT.Copy, HD ** -0.5 if kind == "k" else 1.0)
                        if n >= 2 and c == 0:
                            act.wait_ge(st_stored[u % 2], 16 * st_count(u, u % 2))
                        if c == NCH - 1:
                            link(nc.scalar.activation(SG[:, n, :], samples, fn, scale=scale))
                        nc.scalar.activation(ST[u % 2][:, a:b], src, fn, scale=scale).then_inc(d_free[c], 1)
                    elif kind == "u":
                        if c == 0:
                            act.wait_ge(st_stored[u % 2], 16 * st_count(min(u, N_KQO), u % 2))
                        nc.scalar.activation(ST[u % 2][:, a:b], src, ACT.Copy).then_inc(d_free[c], 1)
                    else:
                        q = NCH * t + c
                        back = [("D", N_MIX - LRU_T + (q - 2) // NCH, (q - 2) % NCH)] if q >= 2 else [("N", NCH - 1, KT - 1)]
                        act.wait_ge(full_ready, full_at[back[0]] + 1)
                        nc.scalar.activation(GT[:, q % 2, :], src, ACT.Gelu_apprx_tanh).then_inc(d_free[c], 1)
                        hi_key(s)
                elif k == "LRUG":
                    t = s[1]
                    for g, (dst, bias) in enumerate(((RG, "ba"), (IG, "bx"))):
                        for c in range(NCH):
                            key = (*s, g, c)
                            wait_full(act, key)
                            nc.scalar.activation(dst[:, c * CH:(c + 1) * CH], bank(key)[:, 0:CH], ACT.Sigmoid,
                                                 bias=col(bias, t)).then_inc(free(key), 1)
                    for c in range(NCH):
                        b, n = use[(*s, 1, c)]
                        act.wait_ge(x_free[b], n + 1)
                    act.wait_ge(lv, 3)
                    nc.scalar.activation(TH[:], RG[:], ACT.Tanh, scale=LS[:, 5, t:t + 1]).then_inc(ah_ready, 1)
                    nc.scalar.activation(AG[:], RG[:], ACT.Exp, scale=LS[:, 4, t:t + 1]).then_inc(ah_ready, 1)
                    act.wait_ge(m2_ready, t + 1)
                    nc.scalar.activation(MU[:], TH[:], ACT.Sqrt).then_inc(mult_ready, 1)
                elif k == "G1":
                    b, n = use[s]
                    act.wait_ge(x_free[b], n + 1)
                    link(nc.scalar.activation(GR[:, R_T, :], GR[:, R_F, :], ACT.Abs))
                    nc.scalar.activation(GR[:, R_T, :], GR[:, R_T, :], ACT.Exp, scale=-1.0).then_inc(ga, 1)
                    act.wait_ge(gv, 1)
                    nc.scalar.activation(GR[:, R_LN, :], GR[:, R_U, :], ACT.Ln).then_inc(ga, 1)
                elif k == "G3":
                    act.wait_ge(nm_ready, 1)
                    nc.scalar.activation(GR[:, R_INT, :], GR[:, R_M, :], ACT.Exp, bias=MPC[:], scale=-1.0).then_inc(int_ready, 1)
                    nc.scalar.activation(GR[:, R_W, :], GR[:, R_A, :], ACT.Exp, bias=GR[:, R_NM, LC - 1:LC]).then_inc(ga, 1)
                    act.wait_ge(gv, 4)
                    nc.scalar.activation(GR[:, R_EM, :], GR[:, R_EM, :], ACT.Exp, scale=-1.0).then_inc(ga, 1)
                elif k == "S":
                    act.wait_ge(ex_ready, s[1] + 1)
                    nc.scalar.activation(EX[:], EX[:], ACT.Exp).then_inc(ex_exp, 1)
                elif k == "AB":
                    act.wait_ge(z_ready, s[1] + 1)
                    nc.scalar.activation(SM4[:, 5, :], SM4[:, 4, :], ACT.Sqrt, bias=EPT[:], scale=1.0 / HD).then_inc(z_root, 1)
                elif k in ("Y", "YS"):
                    hi_key(s)
                elif k == "POOL":
                    for c in range(NCH):
                        hi_key((*s, c))
                elif k == "SMA":
                    act.wait_ge(sma_t, 1)
                    nc.scalar.activation(SR[:, :, 0:2], SR[:, :, 0:2], ACT.Exp).then_inc(sma_e, 1)
                    nc.scalar.activation(SR[:, :, 2], SR[:, :, 3], ACT.Exp, scale=-1.0).then_inc(sma_e, 1)
                elif k == "SMC":
                    act.wait_ge(smc_z, 1)
                    nc.scalar.activation(D32[:, 5:6], D32[:, 4:5], ACT.Sqrt, bias=EPT[0:DEC * HEADS, :], scale=1.0 / HD).then_inc(smc_root, 1)

            def units(first, g, hidden=None, piece=None, square=None):
                for j in range(RAW):
                    u = g * RAW + (first + j)
                    w_hi(u + 1, (first + j + 1 + NADA) % RAW, (first + j + 1) % 2,
                         g * 16 + 16 * ((first + j + 1 + NADA) // RAW + 1))
                    for c in range(NCH):
                        q = NCH * j + c
                        if hidden is not None:
                            act.wait_ge(d_full[c], u + 1)
                            act.wait_ge(full_ready, piece + (q - 1))
                            nc.scalar.activation(GT[:, q % 2, :], DB[c][:, 0:CH], ACT.Relu).then_inc(d_free[c], 1)
                            hi(piece + q, tile(Y_hi, hidden * RAW + j, c * CH, (c + 1) * CH), FU[:, q % FUS, 0:CH])
                        if square is not None:
                            m = hidden_of(first, g, j)
                            act.wait_ge(d_free[c], u + 1)
                            act.wait_ge(ss_done, square + (q - 1))
                            nc.scalar.activation(SQ[:, q % 2, :], tile(X, m, c * CH, (c + 1) * CH), ACT.Square).then_inc(sq_ready, 1)

            def hidden_of(first, g, j):
                return g * RAW + j

            with act.Fori(0, N_OUT // RAW) as g:
                units(N_MIX, g, square=g * PER + SQ_OUT)
            for c in range(NCH):
                root(("NORM", 2, c), P_MIX + c * KT if c else 0)
                for kt in range(KT):
                    h, _, f = norm2_views(c * KT + kt)
                    hi(P_MIX + c * KT + kt, h, f)
            with act.Fori(0, FF_BLOCKS - 1) as b:
                with act.Fori(0, KT // RAW) as g:
                    units(U_FF, b * 4 + g, hidden=g, piece=b * (2 * PER) + g * PER + P_FF)
                with act.Fori(0, KT // RAW) as g:
                    units(U_FF + KT, b * 4 + g)
            with act.Fori(0, KT // RAW) as g:
                units(U_LAST, g, hidden=g, piece=g * PER + P_LAST)
            with act.Fori(0, KT // RAW) as g:
                units(U_LAST + KT, g, square=g * PER + SQ_LAST)
            for c in range(NCH):
                root(("NORM", 3, c), 0)
                if c < NCH - 1:
                    act.wait_ge(fin_ready, (c + 1) * KT)

        @block.vector
        def _(dve):
            step = Rise(dve_step)
            V = nc.vector

            def link(ins):
                step.off += 1
                ins.then_inc(dve_step, 1)
                dve.wait_ge(dve_step, step.at)

            def tell(ins, s, n):
                ins.then_inc(s, 1)
                dve.wait_ge(s, n)

            def slot_free(n):
                if not (isinstance(n, int) and n < FUS):
                    dve.wait_ge(lo_ready, n - (FUS - 1))
                return (n % FUS) if isinstance(n, int) else None

            def put_free(ins, key):
                tell(ins, free(key), use[key][1] + 1)

            for ins in (V.memset(ONE[:], 1.0), V.memset(EPT[:], EPS), V.memset(GTE[:], 0.0), V.memset(MP[:], 0.0),
                        V.memset(VS[0][:, :, HD:HV], 1.0), V.memset(VS[1][:, :, HD:HV], 1.0)):
                ins.then_inc(ones_ready, 1)
            dve.wait_ge(ones_ready, 6)
            dve.wait_ge(sig_c, 1)
            tell(V.tensor_tensor(CTX[:], CTX[:], CTS[:], ALU.mult), c_ready, 1)
            dve.wait_ge(ld_small, 16 * 8)

            def ada(j):
                wait_full(dve, ("ADA", j))
                put_free(V.tensor_scalar(MOD[:, j, :], bank(("ADA", j))[:, 0:DEC + 1], col("b_ada", j), None, ALU.add), ("ADA", j))
                for first, g in ((KT, "g1"), (4 * KT, "g2")):
                    if first <= j < first + KT:
                        link(V.tensor_scalar(MOD[:, j, :], MOD[:, j, :], 1.0, col(g, j - first), ALU.add, ALU.mult))

            def normed(x, c, kt, n, shift, scale, want):
                f = slot_free(n)
                a = c * CH
                last = c == NCH - 1
                link(V.tensor_tensor(FU[:, f, 0:CH], x[:, kt, a:a + CH], RS[:], ALU.mult))
                w = LAST if last else CH
                one = V.tensor_scalar(FU[:, f, 0:w], FU[:, f, 0:w], MOD[:, scale + kt, 0:1], MOD[:, shift + kt, 0:1],
                                      ALU.mult, ALU.add)
                if last:
                    link(one)
                    link(V.tensor_tensor(T8[:], FU[:, f, LAST:CH], MOD[:, scale + kt, 1:], ALU.mult))
                    one = V.tensor_tensor(FU[:, f, LAST:CH], T8[:], MOD[:, shift + kt, 1:], ALU.add)
                tell(one, full_ready, n + 1)

            def inverse_root(norm):
                b, n = use[norm]
                dve.wait_ge(x_free[b], n + 1)
                link(V.reciprocal(RS[:], RS[:]))

            dve.wait_ge(la, 1)
            tell(V.tensor_scalar(LS[:, 1, :], LS[:, 0, :], 1.0, None, ALU.add), lv, 1)
            link(V.tensor_scalar(LS[:, 3, :], LS[:, 1, :], -1.0, None, ALU.add))
            link(V.tensor_tensor(LS[:, 3, :], LS[:, 0, :], LS[:, 3, :], ALU.subtract))
            link(V.reciprocal(LS[:, 4, :], LS[:, 1, :]))
            link(V.tensor_tensor(LS[:, 3, :], LS[:, 3, :], LS[:, 4, :], ALU.mult))
            dve.wait_ge(la, 2)
            link(V.tensor_tensor(LS[:, 3, :], LS[:, 3, :], LS[:, 2, :], ALU.add))
            link(V.tensor_scalar(LS[:, 0, :], col("lam", 0, LRU_T), 0.0, None, ALU.min))
            link(V.tensor_tensor(LS[:, 0, :], LS[:, 0, :], LS[:, 3, :], ALU.subtract))
            tell(V.tensor_scalar(LS[:, 4, :], LS[:, 0, :], 8.0, None, ALU.mult), lv, 2)
            tell(V.tensor_scalar(LS[:, 5, :], LS[:, 0, :], -8.0, None, ALU.mult), lv, 3)
            for j in range(ADA_FIRST):
                ada(j)

            halves = ((0, 64), (64, 128))
            for s in plan:
                k = s[0]
                if k == "NORM":
                    c = s[1]
                    inverse_root(s)
                    for kt in range(KT):
                        normed(X0T, c, kt, full_at[("N", c, kt)], 0, KT, None)
                elif k == "ADA":
                    ada(s[1])
                elif k == "V":
                    t = s[1]
                    wait_full(dve, s)
                    ps = bank(s)
                    if t < NLC:
                        if t >= 2:
                            dve.wait_ge(v_stored[t % 2], 16 * (t // 2))
                        tell(V.tensor_copy(VS[t % 2][:, :, 0:HD], heads(ps[:, 0:HEADS * HD])), v_ready, t + 1)
                        put_free(V.tensor_copy(GTE[:, :, t], ps[:, HEADS * HD:VCOLS]), s)
                    else:
                        tell(V.tensor_copy(VS8[:], ps[0:DEC, 0:HEADS * HD]), v8_ready, 1)
                        put_free(V.tensor_copy(GTE[0:DEC, :, t], ps[0:DEC, HEADS * HD:VCOLS]), s)
                elif k == "G1":
                    wait_full(dve, s)
                    ps = bank(s)
                    link(V.tensor_scalar(GR[:, R_I, :], ps[0:ROWS, 0:LC], GB[:, 0:1], None, ALU.add))
                    put_free(V.tensor_scalar(GR[:, R_F, :], ps[0:ROWS, LC:2 * LC], GB[:, 1:2], None, ALU.add), s)
                    dve.wait_ge(ga, 1)
                    tell(V.tensor_scalar(GR[:, R_U, :], GR[:, R_T, :], 1.0, None, ALU.add), gv, 1)
                    link(V.tensor_scalar(GR[:, R_C, :], GR[:, R_U, :], -1.0, None, ALU.add))
                    link(V.tensor_tensor(GR[:, R_C, :], GR[:, R_T, :], GR[:, R_C, :], ALU.subtract))
                    link(V.reciprocal(GR[:, R_LF, :], GR[:, R_U, :]))
                    link(V.tensor_tensor(GR[:, R_C, :], GR[:, R_C, :], GR[:, R_LF, :], ALU.mult))
                    dve.wait_ge(ga, 2)
                    link(V.tensor_tensor(GR[:, R_C, :], GR[:, R_C, :], GR[:, R_LN, :], ALU.add))
                    link(V.tensor_scalar(GR[:, R_T, :], GR[:, R_F, :], 0.0, None, ALU.min))
                    link(V.tensor_tensor(GR[:, R_LF, :], GR[:, R_T, :], GR[:, R_C, :], ALU.subtract))
                    link(V.tensor_tensor_scan(GR[:, R_BC, :], ONE[0:ROWS, :], GR[:, R_LF, :], 0.0, ALU.mult, ALU.add))
                    link(V.tensor_tensor(GR[:, R_A, :], GR[:, R_I, :], GR[:, R_BC, :], ALU.subtract))
                    tell(V.tensor_tensor_scan(GR[:, R_M, :], GR[:, R_A, :], GR[:, R_A, :], NEG_BIG, ALU.max, ALU.max), gv, 2)
                elif k == "G2":
                    wait_full(dve, s)
                    put_free(V.tensor_copy(BM[:], bank(s)[0:1, 0:2 * ROWS]), s)
                    for h in range(HEADS):
                        r = h * (NLC + 1)
                        one = V.tensor_tensor_scan(MP[:, r + 1:r + 1 + NLC], BM[:, ROWS + r:ROWS + r + NLC], BM[:, r:r + NLC],
                                                   0.0, ALU.max, ALU.add)
                        if h < HEADS - 1:
                            link(one)
                    tell(one, gv, 3)
                elif k == "G3":
                    wait_full(dve, s)
                    put_free(V.tensor_copy(MPC[:], bank(s)[0:ROWS, 0:1]), s)
                    link(V.tensor_scalar(GR[:, R_M, :], GR[:, R_M, :], MPC[:], None, ALU.max))
                    tell(V.tensor_scalar(GR[:, R_NM, :], GR[:, R_M, :], -1.0, None, ALU.mult), nm_ready, 1)
                    tell(V.tensor_tensor(GR[:, R_EM, :], GR[:, R_BC, :], GR[:, R_M, :], ALU.add), gv, 4)
                elif k == "G4":
                    wait_full(dve, s)
                    put_free(V.tensor_copy(COL[:].rearrange("p k r -> p (k r)"), bank(s)[:, 0:4 * ROWS]), s)
                elif k == "LRUC":
                    t = s[1]
                    link(V.memset(XR[t][:, 0:CONV - 1], 0.0))
                    for c in range(NCH):
                        dve.wait_ge(d_free[c], t + 1)
                    w = lambda j: col("conv_w", t * CONV + j)
                    link(V.tensor_scalar(XC[:, 0:SEQ], XR[t][:, CONV - 1:], w(CONV - 1), col("conv_b", t), ALU.mult, ALU.add))
                    link(V.tensor_scalar(XC[:, SEQ:], XS[:, t, :, CONV - 1], w(CONV - 1), col("conv_b", t), ALU.mult, ALU.add))
                    for j in range(CONV - 1):
                        link(V.scalar_tensor_tensor(out=XC[:, 0:SEQ], in0=XR[t][:, j:j + SEQ], scalar=w(j), in1=XC[:, 0:SEQ],
                                                    op0=ALU.mult, op1=ALU.add))
                        link(V.scalar_tensor_tensor(out=XC[:, SEQ:], in0=XS[:, t, :, j], scalar=w(j), in1=XC[:, SEQ:],
                                                    op0=ALU.mult, op1=ALU.add))
                    tell(V.tensor_copy(OUTC[:, t, :], XR[t][:, SEQ:]), xc_ready, t + 1)
                elif k == "LRUG":
                    t = s[1]
                    dve.wait_ge(ah_ready, 2 * (t + 1))
                    link(V.tensor_tensor(MU[:], AG[:], AG[:], ALU.mult))
                    tell(V.scalar_tensor_tensor(out=TH[:], in0=MU[:], scalar=1.0, in1=TH[:], op0=ALU.add, op1=ALU.mult),
                         m2_ready, t + 1)
                    link(V.tensor_tensor(BT[:], IG[:], XC[:], ALU.mult))
                    dve.wait_ge(mult_ready, t + 1)
                    link(V.memset(MU[:, 0:1], 1.0))
                    link(V.tensor_tensor(BT[:], BT[:], MU[:], ALU.mult))
                    link(V.tensor_tensor_scan(HS[t][:, 0:SEQ], AG[:, 0:SEQ], BT[:, 0:SEQ], 0.0, ALU.mult, ALU.add))
                    link(V.tensor_tensor(T8[:], AG[:, SEQ:], col("h0", t * DEC, DEC), ALU.mult))
                    link(V.tensor_tensor(HS[t][:, SEQ:], T8[:], BT[:, SEQ:], ALU.add))
                    tell(V.tensor_copy(OUTL[:, t, :], HS[t][:, SEQ - 1:]), h_ready, t + 1)
                elif k == "D" and UNIT_KIND[s[1]][0] == "gr":
                    _, u, c = s
                    t, n = UNIT_KIND[u][1], full_at[s]
                    dve.wait_ge(d_free[c], u + 1)
                    f = slot_free(n)
                    tell(V.tensor_tensor(FU[:, f, 0:CH], GT[:, (NCH * t + c) % 2, :], HS[t][:, c * CH:(c + 1) * CH], ALU.mult),
                         full_ready, n + 1)
                elif k == "TS":
                    for w in range(2):
                        wait_full(dve, ("TS", w))
                        put_free(V.tensor_copy(QK8[:, w, :], bank(("TS", w))[0:DEC, 0:HEADS * HD]), ("TS", w))
                elif k == "S":
                    c = s[1]
                    dve.wait_ge(ld_kqv[c % 2], 16 * 3 * (c // 2 + 1))
                    if c == 0:
                        tell(V.memset(CN[:], 0.0), cn_ready, 1)
                        dve.wait_ge(ld_dec, 16)
                    dve.wait_ge(ld_nm, 16 * (c + 1))
                    link(V.tensor_tensor(EX[:], NM[:], wide(colh(0, c), LC), ALU.add))
                    tell(V.tensor_tensor(EX[:], EX[:], over(MASK[:], HEADS), ALU.min), ex_ready, c + 1)
                    wait_full(dve, ("KT", c))
                    put_free(V.tensor_tensor(KW[:], heads(bank(("KT", c))[:, 0:HEADS * HD]), wide(colh(1, c), HD), ALU.mult), ("KT", c))
                    dve.wait_ge(ex_exp, c + 1)
                    wait_full(dve, s)
                    put_free(V.tensor_tensor(EX[:], bank(s)[:, 0:HEADS * LC].rearrange("p (h t) -> p h t", h=HEADS), EX[:], ALU.mult), s)
                elif k == "AB":
                    c = s[1]
                    A, B = ("A", c), ("B", c)
                    wait_full(dve, B)
                    put_free(V.tensor_tensor(T1[:], bank(B)[:, 0:HEADS * HV].rearrange("p (h v) -> p h v", h=HEADS),
                                             wide(colh(2, c), HV), ALU.mult), B)
                    wait_full(dve, A)
                    put_free(V.tensor_tensor(NUM[:], bank(A)[:, 0:HEADS * HV].rearrange("p (h v) -> p h v", h=HEADS), T1[:], ALU.add), A)
                    den = NUM[:, :, HD]
                    link(V.scalar_tensor_tensor(out=SM4[:, 0, :], in0=den, scalar=-1.0, in1=den, op0=ALU.mult, op1=ALU.max))
                    link(V.tensor_tensor(SM4[:, 1, :], SM4[:, 0, :], colh(3, c), ALU.max))
                    link(V.reciprocal(SM4[:, 2, :], SM4[:, 1, :]))
                    if c >= 4:
                        dve.wait_ge(x_full["X3"], use[("Y", c - 4)][1] + 1)
                    link(V.tensor_tensor(HM[c % 4][:], NUM[:, :, 0:HD], wide(SM4[:, 2, :], HD), ALU.mult))
                    link(V.tensor_tensor(T1[:, :, 0:HD], HM[c % 4][:], HM[c % 4][:], ALU.mult))
                    tell(V.tensor_reduce(SM4[:, 4, :], T1[:, :, 0:HD], AX_X, ALU.add), z_ready, c + 1)
                    dve.wait_ge(z_root, c + 1)
                    link(V.reciprocal(SM4[:, 6, :], SM4[:, 5, :]))
                    tell(V.tensor_tensor(HM[c % 4][:], HM[c % 4][:], wide(SM4[:, 6, :], HD), ALU.mult), hm_ready, c + 1)
                elif k == "U":
                    c = s[1]
                    link(V.tensor_tensor(CN[:], CN[:], wide(DECB[:].rearrange("p (h c) -> p h c", c=NLC + 1)[:, :, c], HV), ALU.mult))
                    wait_full(dve, s)
                    put_free(V.tensor_tensor(CN[:], bank(s)[0:HD, 0:HEADS * HV].rearrange("p (h v) -> p h v", h=HEADS), CN[:], ALU.add), s)
                elif k in ("Y", "YS"):
                    n = full_at[s]
                    f = slot_free(n)
                    wait_full(dve, s)
                    if k == "Y":
                        dve.wait_ge(ld_o, 16 * (s[1] + 1))
                    w = LC if k == "Y" else DEC
                    for j in range(ML_T):
                        o = OT[:, j, :] if k == "Y" else SG[:, 2 * ML_T + j, :]
                        one = V.scalar_tensor_tensor(out=FU[:, f, j * w:(j + 1) * w], in0=bank(s)[:, j * w:(j + 1) * w],
                                                     scalar=col("ml_g", j), in1=o, op0=ALU.mult, op1=ALU.mult)
                        if j < ML_T - 1:
                            link(one)
                    tell(one, full_ready, n + 1)
                    dve.sem_inc(free(s), 1)
                elif k == "POOL":
                    j = s[1]
                    u = N_MIX - LRU_T - POOL_T + j
                    for c in range(NCH):
                        dve.wait_ge(d_free[c], u + 1)
                    U, A, B = ST[u % 2], PA[j], PB[j]
                    link(V.tensor_copy(UO[:, j, :], U[:, SEQ - PBUF:SEQ]))
                    link(V.tensor_copy(UB[:, j, :, PBUF], U[:, SEQ:]))

                    def doubled(dst, src, by, lo_p, hi_p):
                        link(V.tensor_tensor(dst[lo_p:hi_p, by:SEQ], src[lo_p:hi_p, by:SEQ], src[lo_p:hi_p, 0:SEQ - by], ALU.add))
                        link(V.tensor_copy(dst[lo_p:hi_p, 0:by], src[lo_p:hi_p, 0:by]))

                    doubled(A, U, 1, 0, P)
                    if j == 0:
                        doubled(B, A, 2, 64, P)
                    else:
                        doubled(B, A, 2, 0, P)
                        doubled(A, B, 4, 0, P)
                        doubled(B, A, 8, 64, P)
                    for (p0, p1), src, win in zip(halves, (A, B), WINS[2 * j:2 * j + 2]):
                        link(V.tensor_tensor(src[p0:p1, 0:PBUF], src[p0:p1, 0:PBUF], col("fix", j * PBUF, PBUF, p0, p1), ALU.mult))
                        link(V.scalar_tensor_tensor(out=U[p0:p1, 0:SEQ], in0=src[p0:p1, 0:SEQ], scalar=col("inv_win", j, 1, p0, p1),
                                                    in1=U[p0:p1, 0:SEQ], op0=ALU.mult, op1=ALU.subtract))
                        link(V.tensor_reduce(UM[p0:p1, :], UB[p0:p1, j, :, PBUF + 1 - win:], AX_X, ALU.add))
                        one = V.scalar_tensor_tensor(out=U[p0:p1, SEQ:], in0=UM[p0:p1, :], scalar=col("inv_win", j, 1, p0, p1),
                                                     in1=U[p0:p1, SEQ:], op0=ALU.mult, op1=ALU.subtract)
                        if p0 == 0:
                            link(one)
                    tell(one, u_diff, j + 1)
                    for c in range(NCH):
                        n = full_at[(*s, c)]
                        f = slot_free(n)
                        wait_full(dve, (*s, c))
                        tell(V.tensor_scalar(FU[:, f, 0:CH], bank((*s, c))[:, 0:CH], col("pool_scale", j), None, ALU.mult),
                             full_ready, n + 1)
                        V.sem_inc(free((*s, c)), 1) if False else dve.sem_inc(free((*s, c)), 1)
                elif k == "SMA":
                    link(V.tensor_tensor(SR[:, :, 1], GR[:, R_LF, 0:DEC], M0[:], ALU.add))
                    link(V.tensor_tensor(SR[:, :, 3], SR[:, :, 1], GR[:, R_I, 0:DEC], ALU.max))
                    link(V.tensor_tensor(SR[:, :, 1], SR[:, :, 1], SR[:, :, 3], ALU.subtract))
                    tell(V.tensor_tensor(SR[:, :, 0], GR[:, R_I, 0:DEC], SR[:, :, 3], ALU.subtract), sma_t, 1)
                elif k == "SMB":
                    dve.wait_ge(ld_st, 32)
                    dve.wait_ge(ld_s, 16 * N_LD_S)
                    link(V.tensor_scalar(K32[:], K32[:], S32[:, 0:1], None, ALU.mult))
                    link(V.scalar_tensor_tensor(out=N32[:], in0=N32[:], scalar=S32[:, 1:2], in1=K32[:], op0=ALU.mult, op1=ALU.add))
                    link(V.tensor_tensor(T32[:], N32[:], Q32[:], ALU.mult))
                    link(V.tensor_reduce(D32[:, 0:1], T32[:], AX_X, ALU.add))
                    link(V.tensor_scalar(K128[:], K128[:], S128[:, 0:1], None, ALU.mult))
                    VQ = VH // 4
                    for i in range(4):
                        a, b = i * VQ, (i + 1) * VQ
                        link(V.tensor_tensor(TC[:], wide(V24[:, a:b], HD), over(K128[:], VQ), ALU.mult))
                        link(V.scalar_tensor_tensor(out=CS[:, a:b, :], in0=CS[:, a:b, :], scalar=S128[:, 1:2], in1=TC[:],
                                                    op0=ALU.mult, op1=ALU.add))
                        link(V.tensor_tensor(TC[:], CS[:, a:b, :], over(Q128[:], VQ), ALU.mult))
                        one = V.tensor_reduce(H24[:, a:b], TC[:], AX_X, ALU.add)
                        if i < 3:
                            link(one)
                    tell(one, smb_h, 1)
                elif k == "SMC":
                    dve.wait_ge(ld_h32, 16)
                    link(V.scalar_tensor_tensor(out=D32[:, 1:2], in0=D32[:, 0:1], scalar=-1.0, in1=D32[:, 0:1], op0=ALU.mult, op1=ALU.max))
                    link(V.tensor_tensor(D32[:, 2:3], D32[:, 1:2], S32[:, 2:3], ALU.max))
                    link(V.reciprocal(D32[:, 3:4], D32[:, 2:3]))
                    link(V.tensor_scalar(H32[:], H32[:], D32[:, 3:4], None, ALU.mult))
                    link(V.tensor_tensor(T32[:], H32[:], H32[:], ALU.mult))
                    tell(V.tensor_reduce(D32[:, 4:5], T32[:], AX_X, ALU.add), smc_z, 1)
                    dve.wait_ge(smc_root, 1)
                    link(V.reciprocal(D32[:, 6:7], D32[:, 5:6]))
                    tell(V.tensor_scalar(H32[:], H32[:], D32[:, 6:7], None, ALU.mult), smc_y, 1)

            def units(first, g, residual=None, hidden=None, piece=None):
                for j in range(RAW):
                    u = g * RAW + (first + j)
                    for c in range(NCH):
                        q, a, b = NCH * j + c, c * CH, (c + 1) * CH
                        if hidden is not None:
                            dve.wait_ge(d_free[c], u + 1)
                            slot_free(piece + q)
                            V.tensor_tensor(FU[:, q % FUS, 0:CH], GT[:, q % 2, :], GT[:, q % 2, :], ALU.mult).then_inc(full_ready, 1)
                        else:
                            m_x, m_g = residual[1] * RAW + j, residual[1] * RAW + (residual[0] + j)
                            dve.wait_ge(d_full[c], u + 1)
                            w = CH
                            if c == NCH - 1:
                                w = LAST
                                link(V.tensor_tensor(T8[:], DB[c][:, LAST:CH], tile(MOD, m_g, 1, DEC + 1), ALU.mult))
                                link(V.tensor_tensor(tile(X, m_x, SEQ, TOK), tile(X, m_x, SEQ, TOK), T8[:], ALU.add))
                            tell(V.scalar_tensor_tensor(out=tile(X, m_x, a, a + w), in0=DB[c][:, 0:w], scalar=tile(MOD, m_g, 0, 1),
                                                        in1=tile(X, m_x, a, a + w), op0=ALU.mult, op1=ALU.add), d_free[c], u + 1)

            dve.wait_ge(ld_xres, 16 * KT)
            with dve.Fori(0, N_OUT // RAW) as g:
                step.enter(g, 2 * RAW)
                units(N_MIX, g, residual=(2 * KT, g))
                step.leave(N_OUT // RAW)
            for c in range(NCH):
                inverse_root(("NORM", 2, c))
                for kt in range(KT):
                    normed(X, c, kt, P_MIX + c * KT + kt, 3 * KT, 4 * KT, None)
            before = step.at
            with dve.Fori(0, FF_BLOCKS - 1) as b:
                with dve.Fori(0, KT // RAW) as g:
                    units(U_FF, b * 4 + g, hidden=g, piece=b * (2 * PER) + g * PER + P_FF)
                with dve.Fori(0, KT // RAW) as g:
                    step.base, step.off = b * (4 * RAW) + g * (2 * RAW) + before, 0
                    units(U_FF + KT, b * 4 + g, residual=(5 * KT, g))
                    assert step.off == 2 * RAW
            step.base, step.off = before + (FF_BLOCKS - 1) * 4 * RAW, 0
            with dve.Fori(0, KT // RAW) as g:
                units(U_LAST, g, hidden=g, piece=g * PER + P_LAST)
            with dve.Fori(0, KT // RAW) as g:
                step.enter(g, 2 * RAW)
                units(U_LAST + KT, g, residual=(5 * KT, g))
                step.leave(KT // RAW)
            for c in range(NCH):
                inverse_root(("NORM", 3, c))
                for kt in range(KT):
                    a, b = c * CH, (c + 1) * CH
                    V.scalar_tensor_tensor(out=OUTN[:, kt, a:b], in0=X[:, kt, a:b], scalar=col("gf", kt), in1=RS[:],
                                           op0=ALU.mult, op1=ALU.mult).then_inc(fin_ready, 1)

        @block.tensor
        def _(pe):
            T = nc.tensor

            def take(key):
                b, n = use[key]
                if n:
                    pe.wait_ge(x_free[b], n)
                return XB[b]

            def done(ins, key):
                ins.then_inc(x_full[use[key][0]], 1)

            def ada(j):
                raw = raw_wait(pe, ("ADA", j))
                ps = take(("ADA", j))
                for kt in range(KT):
                    one = T.matmul(ps[:, 0:DEC + 1], RAWW[:, raw, kt * P:(kt + 1) * P], CTX[:, kt, :], start=(kt == 0), stop=(kt == KT - 1))
                done(one, ("ADA", j))

            def sum_squares(key, c, upto):
                pe.wait_ge(ss_done, upto)
                ps = take(key)
                done(T.matmul(ps[:, 0:CH], ONE[:], SS[:, c * CH:(c + 1) * CH], start=True, stop=True), key)

            def dense(u, s, c, hi, lo):
                for kt in range(KT):
                    w_h, w_l = W_hi[:, s, kt * P:(kt + 1) * P], W_lo[:, s, kt * P:(kt + 1) * P]
                    a, b = c * CH, (c + 1) * CH
                    T.matmul(DB[c][:, 0:CH], w_h, hi[:, kt, a:b], start=(kt == 0), stop=False)
                    T.matmul(DB[c][:, 0:CH], w_h, lo[:, kt, a:b], start=False, stop=False)
                    one = T.matmul(DB[c][:, 0:CH], w_l, hi[:, kt, a:b], start=False, stop=(kt == KT - 1))
                one.then_inc(d_full[c], 1)

            pe.wait_ge(c_ready, 1)
            pe.wait_ge(ones_ready, 6)
            pe.wait_ge(ld_small, 16 * 8)
            for j in range(ADA_FIRST):
                ada(j)
            for s in plan:
                k = s[0]
                if k == "NORM":
                    sum_squares(s, s[1], (s[1] + 1) * KT)
                elif k == "ADA":
                    ada(s[1])
                elif k == "V":
                    t = s[1]
                    a = t * LC
                    m = min(LC, TOK - a)
                    pe.wait_ge(wv_lo, 1)
                    pe.wait_ge(lo_ready, KT * ((a + m - 1) // CH + 1))
                    ps = take(s)
                    for kt in range(KT):
                        h, l = H_hi[:, kt, a:a + m], H_lo[:, kt, a:a + m]
                        T.matmul(ps[0:m, 0:VCOLS], h, WV_hi[:, kt, :], start=(kt == 0), stop=False)
                        T.matmul(ps[0:m, 0:VCOLS], h, WV_lo[:, kt, :], start=False, stop=False)
                        one = T.matmul(ps[0:m, 0:VCOLS], l, WV_hi[:, kt, :], start=False, stop=(kt == KT - 1))
                    done(one, s)
                elif k == "D":
                    _, u, c = s
                    pe.wait_ge(w_lo_ready, u + 1)
                    if u:
                        pe.wait_ge(d_free[c], u)
                    dense(u, u % 2, c, H_hi, H_lo)
                elif k == "G1":
                    b, n = use[("V", NLC)]
                    pe.wait_ge(x_free[b], n + 1)
                    ps = take(s)
                    T.transpose(ps[0:ROWS, 0:LC], GTE[:, 0:HEADS, :].rearrange("p g c -> p (g c)"), IDN[:])
                    done(T.transpose(ps[0:ROWS, LC:2 * LC], GTE[:, HEADS:, :].rearrange("p g c -> p (g c)"), IDN[:]), s)
                elif k == "G2":
                    pe.wait_ge(gv, 2)
                    ps = take(s)
                    T.matmul(ps[0:1, 0:ROWS], GR[:, R_BC, LC - 1:LC], IDN[0:ROWS, 0:ROWS], start=True, stop=True)
                    done(T.matmul(ps[0:1, ROWS:2 * ROWS], GR[:, R_M, LC - 1:LC], IDN[0:ROWS, 0:ROWS], start=True, stop=True), s)
                elif k == "G3":
                    pe.wait_ge(gv, 3)
                    done(T.matmul(take(s)[0:ROWS, 0:1], MP[:], ONE[0:1, 0:1], start=True, stop=True), s)
                elif k == "G4":
                    pe.wait_ge(ga, 4)
                    pe.wait_ge(int_ready, 1)
                    ps = take(s)
                    for i, r in enumerate((R_A, R_W, R_INT, R_EM)):
                        one = T.transpose(ps[:, i * ROWS:(i + 1) * ROWS], GR[:, r, :], IDN[0:ROWS, 0:ROWS])
                    done(one, s)
                elif k == "LRUG":
                    t = s[1]
                    pe.wait_ge(xc_ready, t + 1)
                    pe.wait_ge(ld_bdl, 16)
                    for g in range(2):
                        for c in range(NCH):
                            key = (*s, g, c)
                            done(T.matmul(take(key)[:, 0:CH], BDL[:, g * LRU_T + t, :], XC[:, c * CH:(c + 1) * CH], start=True, stop=True), key)
                elif k == "TS":
                    pe.wait_ge(d_free[NCH - 1], 3 + 2 * ML_T)
                    for w in range(2):
                        ps = take(("TS", w))
                        for j in range(ML_T):
                            one = T.transpose(ps[0:DEC, j * P:(j + 1) * P], SG[:, w * ML_T + j, :], IDN[:])
                        done(one, ("TS", w))
                elif k == "S":
                    c = s[1]
                    b = c % 2
                    pe.wait_ge(ld_kqv[b], 16 * 3 * (c // 2 + 1))
                    ps = take(("KT", c))
                    for h in range(HEADS):
                        one = T.transpose(ps[:, h * HD:(h + 1) * HD], K96[b][:, h, :], IDN[0:HD, 0:HD])
                    done(one, ("KT", c))
                    ps = take(s)
                    for h in range(HEADS):
                        one = T.matmul(ps[:, h * LC:(h + 1) * LC], K96[b][:, h, :], Q96[b][:, h, :], start=True, stop=True)
                    done(one, s)
                elif k == "AB":
                    c = s[1]
                    b = c % 2
                    if c == 0:
                        pe.wait_ge(cn_ready, 1)
                    else:
                        bk, n = use[("U", c - 1)]
                        pe.wait_ge(x_free[bk], n + 1)
                    ps = take(("B", c))
                    for h in range(HEADS):
                        one = T.matmul(ps[:, h * HV:(h + 1) * HV], Q96[b][:, h, :], CN[:, h, :], start=True, stop=True)
                    done(one, ("B", c))
                    bk, n = use[("S", c)]
                    pe.wait_ge(x_free[bk], n + 1)
                    ps = take(("A", c))
                    for h in range(HEADS):
                        one = T.matmul(ps[:, h * HV:(h + 1) * HV], EX[:, h, :], VB[b][:, h, :], start=True, stop=True)
                    done(one, ("A", c))
                elif k == "U":
                    c = s[1]
                    bk, n = use[("KT", c)]
                    pe.wait_ge(x_free[bk], n + 1)
                    ps = take(s)
                    for h in range(HEADS):
                        one = T.matmul(ps[0:HD, h * HV:(h + 1) * HV], KW[:, h, :], VB[c % 2][:, h, :], start=True, stop=True)
                    done(one, s)
                elif k == "Y":
                    c = s[1]
                    pe.wait_ge(hm_ready, c + 1)
                    ps = take(s)
                    hm = HM[c % 4][:].rearrange("p h v -> p (h v)")
                    for j in range(ML_T):
                        one = T.transpose(ps[:, j * P:(j + 1) * P], hm[:, j * P:(j + 1) * P], IDN[:])
                    done(one, s)
                elif k == "YS":
                    pe.wait_ge(ld_y8, 16)
                    ps = take(s)
                    for j in range(ML_T):
                        one = T.transpose(ps[:, j * DEC:(j + 1) * DEC], HS8[:, j * P:(j + 1) * P], IDN[0:DEC, 0:DEC])
                    done(one, s)
                elif k == "POOL":
                    j = s[1]
                    u = N_MIX - LRU_T - POOL_T + j
                    pe.wait_ge(u_diff, j + 1)
                    for c in range(NCH):
                        key = (*s, c)
                        done(T.matmul(take(key)[:, 0:CH], BDP[:, j, :], ST[u % 2][:, c * CH:(c + 1) * CH], start=True, stop=True), key)

            def units(first, g, hi, lo, ready):
                for j in range(2):
                    u = g * 2 + (first + j)
                    pe.wait_ge(w_lo_ready, u + 1)
                    for c in range(NCH):
                        pe.wait_ge(lo_ready, ready(c))
                        pe.wait_ge(d_free[c], u)
                        dense(u, (first + j) % 2, c, hi, lo)

            def norm(key, base):
                for c in range(NCH):
                    sum_squares(("NORM", key, c), c, base + NCH * (KT - 1) + c + 1)

            with pe.Fori(0, N_OUT // 2) as g:
                units(N_MIX, g, Y_hi, Y_lo, lambda c: P_MIX)
            norm(2, SQ_OUT)
            with pe.Fori(0, FF_BLOCKS) as b:
                with pe.Fori(0, KT // 2) as g:
                    units(U_FF, b * KT + g, H_hi, H_lo, lambda c: P_MIX + KT * (c + 1))
                with pe.Fori(0, KT // 2) as g:
                    units(U_FF + KT, b * KT + g, Y_hi, Y_lo, lambda c: b * (2 * PER) + (P_FF + NCH * (KT - 1) + c + 1))
            norm(3, SQ_LAST)


def kernel(**inputs):
    import concourse.bacc as bacc
    from concourse.bass_utils import run_bass_kernel_spmd

    a = {k: np.ascontiguousarray(v) for k, v in inputs.items()}
    f32 = np.float32

    def units(w):
        k, n = w.shape
        return w.reshape(k // P, P, n // P, P).transpose(2, 1, 0, 3).reshape(n // P, P, (k // P) * P)

    def tiles(v):
        return v.reshape(-1, P).T

    w_in = a["w_in"][0]
    cut = np.cumsum([384, 384, 384, 384, 384, 384, HEADS, HEADS, 256])
    xr, gr, q, k, v, o, ig, fg, u = np.split(w_in, cut[:-1], axis=1)
    wff2 = a["w_ff2"][0]
    ff1 = units(a["w_ff1"][0])
    mlp = []
    for b in range(FF_BLOCKS):
        mlp += [ff1[b * KT:(b + 1) * KT], units(wff2[b * D:(b + 1) * D])]
    W = np.concatenate([units(xr), units(k), units(q), units(o), units(u), units(gr), units(a["w_out"][0])] + mlp)
    wv = np.concatenate([v, ig, fg], axis=1).reshape(KT, P, VCOLS).transpose(1, 0, 2)
    conv_w = a["conv_w"][0].reshape(CONV, LRU_T, P).transpose(2, 1, 0).reshape(P, LRU_T * CONV)
    h0 = a["state_lru_h"][0].reshape(DEC, LRU_T, P).transpose(2, 1, 0).reshape(P, LRU_T * DEC)
    win = np.array(WINS).reshape(POOL_T, 2).repeat(64, axis=1)
    inv_win = (1.0 / win).T.astype(f32)
    t = np.arange(PBUF)
    fix = (win[:, :, None] / np.minimum(t + 1, win[:, :, None])).transpose(1, 0, 2).reshape(P, POOL_T * PBUF).astype(f32)
    cols = np.concatenate([tiles(a["norm1_g"][0]), tiles(a["norm2_g"][0]), tiles(a["final_g"]), tiles(a["b_ada"][0]), conv_w,
                           tiles(a["conv_b"][0]), tiles(a["lru_ba"][0].reshape(-1)), tiles(a["lru_bx"][0].reshape(-1)),
                           tiles(a["lru_lam"][0]), tiles(a["pool_scale"][0].reshape(-1)), inv_win,
                           tiles(a["mlstm_norm_g"][0].reshape(-1)), fix, h0], axis=1)
    bd = np.zeros((P, 2 * LRU_T + POOL_T, P), f32)
    for i in range(2 * LRU_T):
        t_, e = i // 2, i % 2
        bd[64 * e:64 * e + 64, t_, 64 * e:64 * e + 64] = a["lru_wa"][0, i]
        bd[64 * e:64 * e + 64, LRU_T + t_, 64 * e:64 * e + 64] = a["lru_wx"][0, i]
    for i in range(2 * POOL_T):
        t_, e = i // 2, i % 2
        bd[64 * e:64 * e + 64, 2 * LRU_T + t_, 64 * e:64 * e + 64] = a["pool_w"][0, i]
    conv_state = np.zeros((P, LRU_T, DEC, CONV), f32)
    conv_state[:, :, :, 0:CONV - 1] = a["state_lru_conv"][0].reshape(DEC, CONV - 1, LRU_T, P).transpose(3, 2, 0, 1)
    pool_buf = np.zeros((P, POOL_T, DEC, PBUF + 1), f32)
    pool_buf[:, :, :, 0:PBUF] = a["state_pool"][0].reshape(DEC, PBUF, POOL_T, P).transpose(3, 2, 0, 1)
    gate_bias = np.stack([a["mlstm_bi"][0].repeat(NLC + 1), a["mlstm_bf"][0].repeat(NLC + 1)], axis=1)
    m0 = np.zeros((HEADS, NLC + 1, DEC), f32)
    m0[:, NLC, :] = a["state_mlstm_m"][0].T
    i = np.arange(LC)
    mask = np.where(i[:, None] <= i[None, :], 0.0, NEG_BIG).astype(f32)
    arrays = {
        "x": np.concatenate([a["x_prompt"][0], a["x_sample"][:, 0]]).T,
        "c": np.concatenate([a["c_prompt"], a["c_sample"]]).reshape(DEC + 1, KT, P).transpose(2, 1, 0),
        "W": W, "WADA": units(a["w_ada"][0]), "wv": wv, "cols": cols, "ident": np.eye(P, dtype=f32),
        "bdl": bd[:, :2 * LRU_T], "bdp": bd[:, 2 * LRU_T:],
        "conv_state": conv_state, "pool_buf": pool_buf, "mask": mask, "gate_bias": gate_bias,
        "m0": m0.reshape(ROWS, DEC), "C": a["state_mlstm_C"][0].reshape(P, HD // 4, HD),
        "n": a["state_mlstm_n"][0].reshape(DEC * HEADS, HD),
    }
    outs = {"y": (D, TOK), "lru": (P, LRU_T, DEC + 1), "conv_p": (P, LRU_T, CONV - 1), "conv_s": (P, LRU_T, DEC, CONV),
            "pool_p": (P, POOL_T, PBUF), "pool_s": (P, POOL_T, DEC, PBUF + 1), "C_p": (HD, HEADS, HV), "m_p": (1, ROWS),
            "C_s": (P, HD // 4, HD), "n_s": (DEC * HEADS, HD), "m_s": (ROWS, DEC, 4)}

    nc = bacc.Bacc("TRN2", target_bir_lowering=False, num_devices=1, dynamic_dma_scratch_size=1024)
    arrays = {f"in_{n}": np.ascontiguousarray(v) for n, v in arrays.items()}
    I = {n[3:]: nc.dram_tensor(n, v.shape, mybir.dt.from_np(v.dtype), kind="ExternalInput").ap() for n, v in arrays.items()}
    O = {n: nc.dram_tensor(f"out_{n}", s, F32, kind="ExternalOutput").ap() for n, s in outs.items()}
    build(nc, I, O)
    r = run_bass_kernel_spmd(nc, [arrays], core_ids=[0]).results[0]
    g = {n: r[f"out_{n}"] for n in outs}
    y = g["y"].T
    lru = g["lru"].transpose(2, 1, 0).reshape(DEC + 1, LRU_T * P)
    m_p = g["m_p"].reshape(HEADS, NLC + 1)[:, NLC]
    C_p = g["C_p"].transpose(1, 2, 0)
    return (y[:SEQ][None], y[SEQ:][:, None],
            lru[0][None, None], g["conv_p"].transpose(2, 1, 0).reshape(1, 1, CONV - 1, LRU_T * P),
            C_p[:, :HD][None, None], C_p[:, HD][None, None], m_p[None, None],
            g["pool_p"].transpose(2, 1, 0).reshape(1, 1, PBUF, POOL_T * P),
            lru[1:][None], g["conv_s"][..., 1:].transpose(2, 3, 1, 0).reshape(1, DEC, CONV - 1, LRU_T * P),
            g["C_s"].reshape(1, DEC, HEADS, HD, HD), g["n_s"].reshape(1, DEC, HEADS, HD),
            g["m_s"].reshape(HEADS, NLC + 1, DEC, 4)[:, NLC, :, 3].T[None],
            g["pool_s"][..., 1:].transpose(2, 3, 1, 0).reshape(1, DEC, PBUF, POOL_T * P))
```

```python
from contextlib import ExitStack

import numpy as np

import concourse.bass as bass
from concourse import mybir

ALU = mybir.AluOpType
ACT = mybir.ActivationFunctionType
AX_X = mybir.AxisListType.X
F32 = mybir.dt.float32
F32R = mybir.dt.float32r

P = 128
D = 1024
SEQ = 1024
DEC = 8
TOK = SEQ + DEC
CH = TOK // 3
NCH = 3
LAST = CH - DEC
KT = D // P
LRU_T = 3
ML_T = 3
POOL_T = 2
HEADS, HD = 4, 96
HV = HD + 1
CONV = 4
WINS = (2, 4, 8, 16)
HALVES = ((0, 64), (64, 128))
PBUF = 15
EPS = 1e-6
LC = 128
NLC = SEQ // LC
ROWS = HEADS * (NLC + 1)
VCOLS = HEADS * HD + 2 * HEADS
FF_BLOCKS = 4
NADA = 6 * KT
ADA_FIRST = 2 * KT
N_MIX = 2 * LRU_T + 3 * ML_T + POOL_T
N_KQO = LRU_T + 3 * ML_T
N_OUT = KT
N_FF = FF_BLOCKS * 2 * KT
N_UNITS = N_MIX + N_OUT + N_FF
RAW = 4
FUS = 4
NEG_BIG = -3.0e38

_COLS = {}
_at = 0
for _n, _w in (("g1", KT), ("g2", KT), ("gf", KT), ("b_ada", NADA), ("conv_w", LRU_T * CONV), ("conv_b", LRU_T),
               ("ba", LRU_T), ("bx", LRU_T), ("lam", LRU_T), ("pool_scale", POOL_T), ("inv_win", POOL_T),
               ("ml_g", ML_T), ("fix", POOL_T * PBUF), ("h0", LRU_T * DEC)):
    _COLS[_n] = (_at, _at + _w)
    _at += _w
NCOLS = _at


def plan_mix():
    ada = [("ADA", j) for j in range(ADA_FIRST, NADA)]
    first = [(("ADA", k), ("ADA", KT + k), ("N", 0, k)) for k in range(KT)]
    p = []
    before = {2: [("SQ", 0)], 3: [("WV",)], 4: [("NS", 0)] + [f[2] for f in first[:KT // 2]], 6: [("SQ", 1)]}
    for k, steps in enumerate(first):
        p += before.get(k, []) + list(steps if k >= KT // 2 else steps[:2])
    p += [("NS", 1)] + [("N", 1, k) for k in range(KT)] + [("W0",), ("SQ", 2), ("V", 0), ("V", 1), ("V", 2), ("NS", 2)]
    p += [("N", 2, k) for k in range(KT + 1)] + [("V", t) for t in range(3, NLC + 1)]

    def unit(u, between):
        for c in range(NCH):
            p.append(("D", u, c))
            p.extend(between.get(3 * u + c, []))
            if c < 2 and ada:
                p.append(ada.pop(0))

    after = {0: [("G1",)], 1: [("G2",)], 3: [("G3",)], 4: [("LRUC", 0)], 5: [("G4",)],
             6: [("LRUG", 0)], 7: [("LRUA", 0)], 8: [("LRUM", 0)], 9: [("LRUC", 1)],
             11: [("LRUG", 1)], 12: [("LRUA", 1)], 13: [("LRUM", 1)], 14: [("LRUC", 2)],
             16: [("LRUG", 2)], 17: [("LRUA", 2)], 18: [("LRUM", 2)], 19: [("SMA",)],
             26: [("TS",), ("LD", 0)]}
    o = 3 * N_KQO - 3 * ML_T
    for i, at in enumerate((1, 3, 5, 8, 10, 13, 16, 19)):
        after.setdefault(o + at, []).extend([("S", i)] + [("LD", i + 1)] * (i + 1 < NLC))
        after.setdefault(o + at + 1, []).append(("AB", i))
        after.setdefault(o + at + 2, []).insert(0, ("U", i))
    for at, steps in ((0, [("SMK",)]), (2, [("SMB", 0)]), (3, [("SMB", 1)]), (7, [("SMB", 2)]), (8, [("SMB", 3)]),
                      (9, [("LDO", 0)]), (10, [("SMC",), ("Y", 0)]), (12, [("Y", 1), ("POOLV", 0)]),
                      (14, [("YS",)]), (15, [("Y", 2), ("POOLV", 1)]), (16, [("Y", 3)]), (17, [("POOL", 0), ("POOLD",)]), (18, [("POOL", 1), ("Y", 4)]),
                      (19, [("Y", 5)]), (21, [("Y", 6)]), (22, [("Y", 7)])):
        after.setdefault(o + at, []).extend(steps)
    for u in range(N_MIX):
        unit(u, after)
    assert not ada
    return p


UNIT_KIND = [("xr", t) for t in range(3)] + [("k", t) for t in range(3)] + [("q", t) for t in range(3)] + \
            [("o", t) for t in range(3)] + [("u", t) for t in range(2)] + [("gr", t) for t in range(3)]
AUX = ["X0", "X1", "X2", "X3", "X4"]


def bank_uses(plan):
    count = {b: 0 for b in AUX}
    use = {}

    def add(key, bank):
        use[key] = (bank, count[bank])
        count[bank] += 1

    for s in plan:
        k = s[0]
        if k == "NS":
            add(s, "X0")
        elif k == "V":
            add(s, ("X1", "X2")[s[1] % 2])
        elif k == "ADA":
            add(s, "X3" if (s[1] < KT if s[1] < ADA_FIRST else s[1] % 2 == 0) else "X4")
        elif k in ("G1", "G2", "G3", "G4", "Y", "YS"):
            add(s, "X3")
        elif k == "TS":
            for w in range(2):
                add(("TS", w), ("X3", "X4")[w])
        elif k == "LRUG":
            for g in range(2):
                for c in range(NCH):
                    add((*s, g, c), ("X0", "X1", "X2")[c])
        elif k == "S":
            add(("S", s[1]), "X0")
            add(("KT", s[1]), "X3")
        elif k == "AB":
            add(("A", s[1]), "X1")
            add(("B", s[1]), "X2")
        elif k == "U":
            add(s, "X0")
        elif k == "POOL":
            for c in range(NCH):
                add((*s, c), ("X1", "X2")[c % 2])
    for n in (2, 3):
        for c in range(NCH):
            add(("NORM", n, c), ("X0", "X1", "X2")[c])
    return use


class Rise:

    def __init__(self, sem):
        self.sem, self.base, self.off = sem, 0, 0

    @property
    def at(self):
        return self.base + self.off

    def enter(self, i, per):
        self.before, self.per = self.at, per
        self.base, self.off = self.before + i * per, 0

    def leave(self, times):
        assert self.off == self.per, (self.off, self.per)
        self.base, self.off = self.before + times * self.per, 0



def norm_target(c, kt):
    return ("HS", 0, SEQ, DEC) if kt == KT else ("H", kt, c * CH, LAST if c == NCH - 1 else CH)


def plan_pieces(plan):
    out = []
    for s in plan:
        if s[0] == "N":
            out.append((s, norm_target(s[1], s[2])))
        elif s[0] == "D" and UNIT_KIND[s[1]][0] == "gr":
            out.append((s, ("Y", UNIT_KIND[s[1]][1], s[2] * CH, CH)))
        elif s[0] == "Y":
            out.append((s, ("Y3", LRU_T, s[1] * LC, LC)))
        elif s[0] == "YS":
            out.append((s, ("Y3", LRU_T, SEQ, DEC)))
        elif s[0] == "POOL":
            out += [((*s, c), ("Y", LRU_T + ML_T + s[1], c * CH, CH)) for c in range(NCH)]
    return out


def build(nc, I, O):
    plan = plan_mix()
    use = bank_uses(plan)
    pieces = plan_pieces(plan)
    full_at = {k: n for n, (k, _) in enumerate(pieces)}
    target = dict(pieces)
    P_MIX = len(pieces)
    P_NORM = NCH * KT + 1
    P_FF = P_MIX + P_NORM
    raw_seq = []
    for s in plan:
        if s[0] == "D" and s[2] == 0:
            raw_seq.append(("W", s[1]))
        elif s[0] == "ADA":
            raw_seq.append(s)
    assert len(raw_seq) == N_MIX + NADA
    raw_seq += [("W", u) for u in range(N_MIX, N_MIX + RAW)]
    raw_at = {k: n for n, k in enumerate(raw_seq)}

    SHIFTED = KT - 2
    PER = NCH * RAW
    N_SQ = NCH * KT
    U_FF = N_MIX + N_OUT
    U_LAST = U_FF + (FF_BLOCKS - 1) * 2 * KT
    U_MID, P_MID = U_FF + 2 * KT, P_FF + NCH * KT
    P_LAST = P_FF + (FF_BLOCKS - 1) * NCH * KT
    N_LD_S = 1 + 4 + 2 * (4 + 1) + 1
    with ExitStack() as ctx:
        SLOT = TOK * 4
        top = [nc.sbuf_base + (-nc.sbuf_base) % 32]

        def region(size):
            a = top[0]
            top[0] += size + (-size) % 32
            return a

        def at(name, shape, off, dt=F32):
            return nc.alloc_sbuf_tensor_at(name, shape, dt, offset=off)

        def new(name, shape, dt=F32):
            return at(name, shape, region(int(np.prod(shape[1:])) * 4), dt)

        rH = top[0]
        H_hi = new("H_hi", [P, KT, TOK], F32R)
        H_lo = new("H_lo", [P, KT, TOK], F32R)
        rY = region(2 * KT * SLOT)
        Y_hi = at("Y_hi", [P, KT, TOK], rY, F32R)
        Y_lo = at("Y_lo", [P, KT, TOK], rY + KT * SLOT, F32R)
        RAWW = new("RAWW", [P, RAW, KT * P])
        W_hi = new("W_hi", [P, 2, KT * P], F32R)
        W_lo = new("W_lo", [P, 2, KT * P], F32R)
        rX = region(KT * SLOT)
        X = at("X", [P, KT, TOK], rX)

        slot = [rY + k * SLOT for k in range(2 * KT)]
        X0T = at("X0T", [P, KT, TOK], rY)
        WV_hi = at("WV_hi", [P, KT, VCOLS], slot[8], F32R)
        XR = [at(f"XR{t}", [P, SEQ + CONV - 1], slot[3 + t]) for t in range(3)]
        XC, RG = at("XC", [P, TOK], slot[6]), at("RG", [P, TOK], slot[7])
        IG, AG, TH = at("IG", [P, TOK], slot[11]), at("AG", [P, TOK], slot[12]), at("TH", [P, TOK], slot[13])
        BT, MU = at("BT", [P, TOK], slot[14]), at("MU", [P, TOK], slot[15])
        HS = [at(f"HS{t}", [P, TOK], slot[8 + t]) for t in range(3)]
        PA = [at(f"PA{j}", [P, TOK], slot[1 + j]) for j in range(2)]
        PB = [at(f"PB{j}", [P, TOK], slot[6 + j]) for j in range(2)]
        OUTN = at("OUTN", [P, KT, TOK], rY)

        WV_raw = at("WV_raw", [P, KT, VCOLS], rX)
        WV_lo = at("WV_lo", [P, KT, VCOLS], rX + KT * VCOLS * 4, F32R)
        VS = [at(f"VS{b}", [P, HEADS, HV], rX + 2 * KT * VCOLS * 4 + 1568 * b) for b in range(2)]
        inx_at = [rX]

        def inx(name, shape):
            a, size = inx_at[0], int(np.prod(shape[1:])) * 4
            inx_at[0] += size + (-size) % 32
            assert inx_at[0] <= rX + KT * SLOT, name
            return at(name, shape, a)

        K96 = [inx(f"K96_{b}", [HD, HEADS, LC]) for b in range(2)]
        Q96 = [inx(f"Q96_{b}", [HD, HEADS, LC]) for b in range(2)]
        VB = [inx(f"VB{b}", [P, HEADS, HV]) for b in range(2)]
        NM, EX = inx("NM", [P, HEADS, LC]), inx("EX", [P, HEADS, LC])
        KW, CN = inx("KW", [P, HEADS, HD]), inx("CN", [HD, HEADS, HV])
        T1, NUM = inx("T1", [P, HEADS, HV]), inx("NUM", [P, HEADS, HV])
        HM = [inx(f"HM{b}", [P, HEADS, HD]) for b in range(4)]
        OT = inx("OT", [P, ML_T, LC])

        FU = new("FU", [P, FUS, 3 * LC])
        ST = [new(f"ST{b}", [P, TOK]) for b in range(2)]
        rN = region(14 * LC * 4)
        SQ, SS = at("SQ", [P, 2, CH], rN), at("SS", [P, TOK], rN + 2 * CH * 4)
        GT = at("GT", [P, 2, CH], rN)
        MOD, CTX = new("MOD", [P, NADA, DEC + 1]), new("CTX", [P, KT, DEC + 1])
        CTS = at("CTS", [P, KT, DEC + 1], rH)
        COLS, IDN, ONE = new("COLS", [P, NCOLS]), new("IDN", [P, P]), new("ONE", [P, P])
        EPT, LS = new("EPT", [P, 1]), new("LS", [P, 6, LRU_T])
        BG2 = new("BG2", [P, KT])
        XS, OUTC = new("XS", [P, LRU_T, DEC, CONV]), new("OUTC", [P, LRU_T, CONV - 1])
        OUTL = new("OUTL", [P, LRU_T, DEC + 1])
        SG = inx("SG", [P, 3 * ML_T, DEC])
        BDL = at("BDL", [P, 2 * LRU_T, P], slot[0])
        BDP = new("BDP", [P, POOL_T, P])
        UB, UO, UM = new("UB", [P, POOL_T, DEC, PBUF + 1]), new("UO", [P, POOL_T, PBUF]), new("UM", [P, DEC])
        MASK, T8 = inx("MASK", [P, LC]), new("T8", [P, DEC])
        GTE = inx("GTE", [P, 2 * HEADS, NLC + 1])
        VS8 = inx("VS8", [DEC, HEADS * HD])
        QK8 = at("QK8", [DEC, 2, HEADS * HD], slot[14])
        HS8 = at("HS8", [DEC, HEADS * HD], slot[14] + 2 * HEADS * HD * 4)
        GR = at("GR", [ROWS, 14, LC], rN)
        R_I, R_F, R_T, R_U, R_LN, R_C, R_LF, R_BC, R_A, R_INT, R_M, R_NM, R_W, R_EM = range(14)
        GB, M0, SR = new("GB", [ROWS, 2]), new("M0", [ROWS, DEC]), new("SR", [ROWS, DEC, 4])
        MPC, BM, MP = new("MPC", [ROWS, 1]), new("BM", [1, 2 * ROWS]), new("MP", [1, ROWS])
        COL, DECB = inx("COL", [P, 4, ROWS]), inx("DECB", [HD, ROWS])
        SM4 = new("SM4", [P, 8, HEADS])
        VH = HD // 4
        CS, TC = at("CS", [P, VH, HD], slot[11]), at("TC", [P, VH // 4, HD], slot[11] + VH * HD * 4)
        small = [slot[14] + 3 * HEADS * HD * 4 + i * HD * 4 for i in range(8)]
        K128, Q128 = at("K128", [P, HD], small[0]), at("Q128", [P, HD], small[1])
        V24, H24, S128 = at("V24", [P, VH], small[7]), at("H24", [P, VH], small[7] + 96), at("S128", [P, 4], small[7] + 192)
        K32, Q32, N32, H32, T32 = (at(n, [DEC * HEADS, HD], small[2 + i]) for i, n in enumerate(("K32", "Q32", "N32", "H32", "T32")))
        S32, D32 = at("S32", [DEC * HEADS, 4], small[7] + 224), at("D32", [DEC * HEADS, 8], small[7] + 256)
        assert top[0] <= nc.sbuf_usable_end, (top[0], nc.sbuf_usable_end)

        DB = [ctx.enter_context(nc.psum_tensor(f"D{c}", [P, 512], F32)) for c in range(NCH)]
        XB = {n: ctx.enter_context(nc.psum_tensor(n, [P, 512], F32)) for n in AUX}

        def dram(name, shape):
            return nc.dram_tensor(name, shape, F32).ap()

        k_d, q_d, o_d = (dram(n, [ML_T * P, SEQ]) for n in ("k_d", "q_d", "o_d"))
        v_d = dram("v_d", [NLC, P, HEADS * HV])
        sv_d, sk_d, sq_d, sh_d, sy_d = (dram(n, [DEC, HEADS * HD]) for n in ("sv_d", "sk_d", "sq_d", "sh_d", "sy_d"))
        nm_d, dec_d, sr_d = dram("nm_d", [ROWS, LC]), dram("dec_d", [ROWS, 1]), dram("sr_d", [DEC, HEADS, 4])

        def col(name, k=0, n=1, p0=0, p1=P):
            a = _COLS[name][0] + k
            return COLS[p0:p1, a:a + n]

        def heads(ap):
            return ap.rearrange("p (h d) -> p h d", h=HEADS)

        def colh(k, c):
            return COL[:, k, :].rearrange("p (h c) -> p h c", c=NLC + 1)[:, :, c]

        def wide(ap, n):
            return ap.unsqueeze(2).to_broadcast([ap.shape[0], ap.shape[1], n])

        def over(ap, n):
            return ap.unsqueeze(1).to_broadcast([ap.shape[0], n, ap.shape[1]])

        def tile(t, i, a, b):
            if isinstance(i, int):
                return t[:, i, a:b]
            return t[:, bass.ds(i, 1), a:b].rearrange("p a n -> p (a n)")

        def sem(name):
            return ctx.enter_context(nc.semaphore(name))

        d_full = [sem(f"dense{c}_full") for c in range(NCH)]
        d_free = [sem(f"dense{c}_free") for c in range(NCH)]
        x_full = {b: sem(f"{b}_full") for b in AUX}
        x_free = {b: sem(f"{b}_free") for b in AUX}
        raw_in = [sem(f"raw{r}_in") for r in range(RAW)]
        w_hi_ready, w_lo_ready = sem("w_hi_ready"), sem("w_lo_ready")
        full_ready = sem("full_ready")
        hi_ready, lo_ready = sem("hi_ready"), sem("lo_ready")
        sq_ready, ss_done = sem("sq_ready"), sem("ss_done")
        ss1_done = sem("ss1_done")
        ss_zero = sem("ss_zero")
        act_step, dve_step = sem("act_step"), sem("dve_step")
        ld_x = [sem(f"ld_x{c}") for c in range(NCH)]
        pool_step = sem("pool_step")
        u_kept, u_small = sem("u_kept"), sem("u_small")
        u1_diff, bg_ready = sem("u1_diff"), sem("bg_ready")
        ld_cols, ld_small, ld_c, ld_wv = sem("ld_cols"), sem("ld_small"), sem("ld_c"), sem("ld_wv")
        ld_xres = [sem(f"ld_xres{m}") for m in range(KT)]
        ones_ready, sig_c, c_ready = sem("ones_ready"), sem("sig_c"), sem("c_ready")
        wv_hi, wv_lo = sem("wv_hi"), sem("wv_lo")
        v_ready, v8_ready, v8_stored = sem("v_ready"), sem("v8_ready"), sem("v8_stored")
        v_stored = [sem(f"v_stored{b}") for b in range(2)]
        st_stored = [sem(f"st_stored{b}") for b in range(2)]
        ga, gv = sem("gate_rows_act"), sem("gate_rows_dve")
        nm_ready, nm_stored, int_ready, dec_stored, ld_dec = (sem(n) for n in (
            "nm_ready", "nm_stored", "int_ready", "dec_stored", "ld_dec"))
        la, lv = sem("lam_act"), sem("lam_dve")
        xc_ready, ah_ready, m2_ready, mult_ready, h_ready = (sem(n) for n in (
            "xc_ready", "ah_ready", "m2_ready", "mult_ready", "h_ready"))
        ts_stored, u_diff = sem("ts_stored"), sem("u_diff")
        ld_kqv = [sem(f"ld_kqv{b}") for b in range(2)]
        ld_nm, ld_o, ld_mask = sem("ld_nm"), sem("ld_o"), sem("ld_mask")
        ex_ready, ex_exp, cn_ready = sem("ex_ready"), sem("ex_exp"), sem("cn_ready")
        z_ready, z_root, hm_ready = sem("z_ready"), sem("z_root"), sem("hm_ready")
        sma_t, sma_e, sr_stored = sem("sma_t"), sem("sma_e"), sem("sr_stored")
        ld_st, ld_s, ld_bdl = sem("ld_state"), sem("ld_s"), sem("ld_bdl")
        smb_h, h_stored, ld_h32 = sem("smb_h"), sem("h_stored"), sem("ld_h32")
        smc_z, smc_root, smc_y, y_stored, ld_y8 = (sem(n) for n in ("smc_z", "smc_root", "smc_y", "y_stored", "ld_y8"))
        fin_ready, out_done = sem("fin_ready"), sem("out_done")
        c_out, s_out = sem("c_out"), sem("s_out")

        def st_count(u, b):
            return sum(v % 2 == b for v in range(LRU_T, u))

        def raw_wait(e, key):
            n = raw_at[key]
            e.wait_ge(raw_in[n % RAW], 16 * (n // RAW + 1))
            return n % RAW

        def raw_slot(u):
            return raw_at[("W", u)] % RAW

        def load_raw(e, n):
            kind, j = raw_seq[n]
            e.dma_start(RAWW[:, n % RAW, :], I["WADA" if kind == "ADA" else "W"][j]).then_inc(raw_in[n % RAW], 16)

        def mod_ready(e):
            for j in (NADA - 2, NADA - 1):
                b, n = use[("ADA", j)]
                e.wait_ge(x_free[b], n + 1)

        def bank(key):
            return XB[use[key][0]]

        def wait_full(e, key):
            b, n = use[key]
            e.wait_ge(x_full[b], n + 1)

        def free(key):
            return x_free[use[key][0]]

        block = ctx.enter_context(nc.Block())

        @block.sync
        def _(sp):
            x_v = I["x"].rearrange("(k p) t -> p k t", p=P)

            def load_x(c):
                sp.dma_start(X0T[:, :, c * CH:(c + 1) * CH], x_v[:, :, c * CH:(c + 1) * CH]).then_inc(ld_x[c], 16)

            def load_o(c):
                sp.dma_start(OT[:], o_d.rearrange("(j p) t -> p j t", p=P)[:, :, c * LC:(c + 1) * LC]).then_inc(ld_o, 16)

            sp.dma_start(CTX[:], I["c"]).then_inc(ld_c, 16)
            sp.dma_start(COLS[:], I["cols"]).then_inc(ld_cols, 16)
            for n in range(ADA_FIRST + RAW):
                if n >= RAW:
                    wait_full(sp, raw_seq[n - RAW])
                load_raw(sp, n)
                if n == RAW - 1:
                    load_x(0)
                elif n == 2 * RAW - 1:
                    sp.dma_start(WV_raw[:], I["wv"]).then_inc(ld_wv, 16)
                elif n == 2 * RAW + 1:
                    load_x(1)
                elif n == 4 * RAW - 2:
                    load_x(2)
            for dst, name in ((IDN, "ident"), (BDP, "bdp"), (XS, "conv_state"), (UB, "pool_buf"), (GB, "gate_bias"), (M0, "m0")):
                sp.dma_start(dst[:], I[name]).then_inc(ld_small, 16)
            for s in plan:
                k = s[0]
                if k == "V":
                    t = s[1]
                    if t < NLC:
                        sp.wait_ge(v_ready, t + 1)
                        sp.dma_start(v_d[t], VS[t % 2][:].rearrange("p h v -> p (h v)")).then_inc(v_stored[t % 2], 16)
                    else:
                        sp.wait_ge(v8_ready, 1)
                        sp.dma_start(sv_d, VS8[:]).then_inc(v8_stored, 16)
                elif k == "G1":
                    sp.wait_ge(full_ready, P_NORM)
                    sp.dma_start(BDL[:], I["bdl"]).then_inc(ld_bdl, 16)
                elif k == "G3":
                    sp.wait_ge(nm_ready, 1)
                    sp.dma_start(nm_d, GR[:, R_NM, :]).then_inc(nm_stored, 16)
                    sp.wait_ge(int_ready, 1)
                    sp.dma_start(dec_d, GR[:, R_INT, LC - 1:LC]).then_inc(dec_stored, 16)
                    sp.wait_ge(dec_stored, 16)
                    sp.dma_start(DECB[:], dec_d.rearrange("r a -> (r a)").partition_broadcast(HD)).then_inc(ld_dec, 16)
                elif k == "D" and s[2] == NCH - 1:
                    u = s[1]
                    kind, t = UNIT_KIND[u]
                    if kind in ("k", "q", "o"):
                        for c in range(NCH):
                            sp.wait_ge(d_free[c], u + 1)
                        dst = {"k": k_d, "q": q_d, "o": o_d}[kind]
                        sp.dma_start(dst[t * P:(t + 1) * P, :], ST[u % 2][:, 0:SEQ]).then_inc(st_stored[u % 2], 16)
                elif k == "TS":
                    for w in range(2):
                        b, n = use[("TS", w)]
                        sp.wait_ge(x_free[b], n + 1)
                    sp.dma_start(sk_d, QK8[:, 0, :]).then_inc(ts_stored, 16)
                    sp.dma_start(sq_d, QK8[:, 1, :]).then_inc(ts_stored, 16)
                elif k == "LD":
                    c = s[1]
                    b = c % 2
                    if c == 0:
                        for i in range(2):
                            sp.wait_ge(st_stored[i], 16 * ML_T)
                            sp.wait_ge(v_stored[i], 16 * NLC // 2)
                        sp.wait_ge(nm_stored, 16)
                        sp.wait_ge(v8_ready, 1)
                        sp.dma_start(MASK[:], I["mask"]).then_inc(ld_mask, 16)
                    if c >= 2:
                        wait_full(sp, ("U", c - 2))
                        wait_full(sp, ("B", c - 2))
                    for src, dst in ((k_d, K96[b]), (q_d, Q96[b])):
                        sp.dma_start(dst[:], src.rearrange("(h d) t -> d h t", d=HD)[:, :, c * LC:(c + 1) * LC]).then_inc(ld_kqv[b], 16)
                    sp.dma_start(VB[b][:].rearrange("p h v -> p (h v)"), v_d[c]).then_inc(ld_kqv[b], 16)
                    if c >= 1:
                        sp.wait_ge(ex_ready, c)
                    sp.dma_start(NM[:], nm_d.rearrange("(h c) t -> c h t", c=NLC + 1)[c].partition_broadcast(P)).then_inc(ld_nm, 16)
                elif k == "SMA":
                    sp.wait_ge(h_ready, LRU_T)
                    sp.dma_start(CS[:], I["C"]).then_inc(ld_st, 16)
                    sp.dma_start(N32[:], I["n"]).then_inc(ld_st, 16)
                    sp.wait_ge(sma_e, 2)
                    sp.dma_start(sr_d.rearrange("b h k -> h b k"), SR[NLC::NLC + 1, :, :]).then_inc(sr_stored, 16)
                    sp.dma_start(O["m_s"], SR[:]).then_inc(out_done, 16)
                    sp.wait_ge(sr_stored, 16)
                    rows = sr_d.rearrange("b h k -> (b h) k")
                    sp.dma_start(S32[:], rows).then_inc(ld_s, 16)
                    for q in range(4):
                        sp.dma_start(S128[q::4, :], rows).then_inc(ld_s, 16)
                elif k == "SMK":
                    sp.wait_ge(ts_stored, 32)
                    sp.wait_ge(v8_stored, 16)
                    for src, wide_t, t in ((sk_d, K128, K32), (sq_d, Q128, Q32)):
                        for q in range(4):
                            sp.dma_start(wide_t[q::4, :], src.rearrange("b (h d) -> (b h) d", d=HD)).then_inc(ld_s, 16)
                        sp.dma_start(t[:], src.rearrange("b (h d) -> (b h) d", d=HD)).then_inc(ld_s, 16)
                    sp.dma_start(V24[:], sv_d.rearrange("b (x v) -> (b x) v", v=VH)).then_inc(ld_s, 16)
                elif s == ("SMB", 3):
                    sp.wait_ge(smb_h, 1)
                    sp.dma_start(sh_d.rearrange("b (x v) -> (b x) v", v=VH), H24[:]).then_inc(h_stored, 16)
                    sp.wait_ge(h_stored, 16)
                    sp.dma_start(H32[:], sh_d.rearrange("b (h d) -> (b h) d", d=HD)).then_inc(ld_h32, 16)
                    sp.dma_start(O["C_s"], CS[:]).then_inc(s_out, 16)
                    sp.dma_start(O["n_s"], N32[:]).then_inc(s_out, 16)
                elif k == "SMC":
                    sp.wait_ge(smc_y, 1)
                    sp.dma_start(sy_d.rearrange("b (h d) -> (b h) d", d=HD), H32[:]).then_inc(y_stored, 16)
                    sp.wait_ge(y_stored, 16)
                    sp.dma_start(HS8[:], sy_d).then_inc(ld_y8, 16)
                elif k == "LDO":
                    for i in range(2):
                        sp.wait_ge(st_stored[i], 16 * st_count(N_KQO, i))
                    load_o(0)
                elif k == "Y" and s[1] < NLC - 1:
                    sp.wait_ge(full_ready, full_at[s] + 1)
                    load_o(s[1] + 1)
            def load_residual(m):
                sp.dma_start(X[:, m, :], I["x"][m * P:(m + 1) * P, :]).then_inc(ld_xres[m], 16)

            wait_full(sp, ("A", NLC - 1))
            wait_full(sp, ("U", NLC - 1))
            for m in range(4):
                load_residual(m)
            b, n = use[("U", NLC - 1)]
            sp.wait_ge(x_free[b], n + 1)
            sp.dma_start(O["C_p"], CN[:]).then_inc(c_out, 16)
            sp.wait_ge(full_ready, full_at[("Y", NLC - 1)] + 1)
            sp.wait_ge(c_out, 16)
            for m in range(4, KT):
                load_residual(m)
            sp.dma_start(O["m_p"], MP[:]).then_inc(out_done, 16)
            sp.wait_ge(h_ready, LRU_T)
            sp.dma_start(O["lru"], OUTL[:]).then_inc(out_done, 16)
            sp.dma_start(O["conv_p"], OUTC[:]).then_inc(out_done, 16)
            sp.dma_start(O["conv_s"], XS[:]).then_inc(out_done, 16)
            sp.wait_ge(u_small, POOL_T)
            sp.dma_start(O["pool_p"], UO[:]).then_inc(out_done, 16)
            sp.dma_start(O["pool_s"], UB[:]).then_inc(out_done, 16)
            with sp.Fori(0, (N_OUT + N_FF - RAW) // RAW) as g:
                for j in range(RAW):
                    r = (N_MIX + NADA + j) % RAW
                    sp.wait_ge(w_lo_ready, g * RAW + (N_MIX + j + 1))
                    sp.dma_start(RAWW[:, r, :], I["W"][bass.ds(g * RAW + (N_MIX + RAW + j), 1)].rearrange("a p n -> p (a n)")
                                 ).then_inc(raw_in[r], 16)
            sp.wait_ge(w_lo_ready, N_UNITS - RAW + 1)
            sp.dma_start(RAWW[:, (N_UNITS + NADA) % RAW, :], I["W"][N_UNITS - 1]).then_inc(raw_in[(N_UNITS + NADA) % RAW], 16)
            y_v = O["y"].rearrange("(k p) t -> p k t", p=P)
            for c in range(NCH):
                for kt in range(KT):
                    sp.wait_ge(fin_ready, c * KT + kt + 1)
                    sp.dma_start(y_v[:, kt, c * CH:(c + 1) * CH], OUTN[:, kt, c * CH:(c + 1) * CH]).then_inc(out_done, 16)
            sp.wait_ge(s_out, 32)
            sp.wait_ge(out_done, 16 * (7 + NCH * KT))

        def piece_views(where, f):
            kind, kt, t0, n = where
            hi, lo = (Y_hi, Y_lo) if kind in ("Y", "Y3") else (H_hi, H_lo)
            if kind in ("Y3", "HS"):
                w = ML_T if kind == "Y3" else KT
                return hi[:, kt:kt + w, t0:t0 + n], lo[:, kt:kt + w, t0:t0 + n], \
                    FU[:, f, 0:w * n].rearrange("p (j t) -> p j t", j=w)
            return hi[:, kt, t0:t0 + n], lo[:, kt, t0:t0 + n], FU[:, f, 0:n]

        def views(key):
            return piece_views(target[key], full_at[key] % FUS)

        def norm_pieces(c):
            return range(KT + 1 if c == NCH - 1 else KT)

        def norm2_piece(c, kt):
            n = P_MIX + c * KT + kt
            return n, *piece_views(norm_target(c, kt), n % FUS)

        def norm_done(c):
            return (c + 1) * KT + (c == NCH - 1)

        def u_unit(j):
            return N_MIX - LRU_T - POOL_T + j

        def pool_windows(e, j, link):
            U, A, B = ST[u_unit(j) % 2], PA[j], PB[j]

            def doubled(dst, src, by, p0):
                link(e.tensor_tensor(dst[p0:P, by:SEQ], src[p0:P, by:SEQ], src[p0:P, 0:SEQ - by], ALU.add))
                link(e.tensor_copy(dst[p0:P, 0:by], src[p0:P, 0:by]))

            upper = HALVES[1][0]
            doubled(A, U, 1, 0)
            if j == 0:
                doubled(B, A, 2, upper)
            else:
                doubled(B, A, 2, 0)
                doubled(A, B, 4, 0)
                doubled(B, A, 8, upper)
            for (p0, p1), src in zip(HALVES, (A, B)):
                link(e.tensor_tensor(src[p0:p1, 0:PBUF], src[p0:p1, 0:PBUF], col("fix", j * PBUF, PBUF, p0, p1), ALU.mult))

        def steps_of(paired=None):
            out = []
            for p in range(2):
                if p == paired:
                    out += [(2 * p + k % 2, k // 2, k % 3, 2 * p + k // 3) for k in range(6)]
                else:
                    out += [(j, c, c, j) for j in (2 * p, 2 * p + 1) for c in range(NCH)]
            return out

        def next_parts(paired):
            out = {}
            for p in range(2):
                if p or paired != 0:
                    out[6 * p] = (2 * p + 1, NCH - 1, 2 * p - 1)
                out[6 * p + 5 if p == paired else 6 * p + 3] = (2 * p + 2, 1 if p == paired else NCH - 1, 2 * p + (p == paired))
            return out

        WOVEN = ([], [], [], range(0, 3), range(3, 6), range(6, KT))
        FF_SLOT = [(P_FF + q) % FUS for q in range(PER)]

        @block.gpsimd
        def _(pool):
            def w_lo(u, raw, s):
                pool.wait_ge(w_hi_ready, u + 1)
                nc.gpsimd.tensor_tensor(W_lo[:, s, :], RAWW[:, raw, :], W_hi[:, s, :].bitcast(F32),
                                        ALU.subtract).then_inc(w_lo_ready, 1)

            def lo(n, hi_v, lo_v, fu_v):
                pool.wait_ge(hi_ready, n + 1)
                nc.gpsimd.tensor_tensor(lo_v, fu_v, hi_v.bitcast(F32), ALU.subtract).then_inc(lo_ready, 1)

            steps = Rise(pool_step)

            def link(ins):
                steps.off += 1
                ins.then_inc(pool_step, 1)
                pool.wait_ge(pool_step, steps.at)

            def add_square(n, c, s):
                pool.wait_ge(sq_ready, n + (N_SQ + 1))
                nc.gpsimd.tensor_tensor(SS[:, c * CH:(c + 1) * CH], SS[:, c * CH:(c + 1) * CH], SQ[:, s, :],
                                        ALU.add).then_inc(ss_done, 1)
                pool.wait_ge(ss_done, n + 1)

            nc.gpsimd.memset(SS[:], 0.0).then_inc(ss_zero, 1)
            for s in plan:
                k = s[0]
                if k == "WV":
                    pool.wait_ge(wv_hi, 1)
                    nc.gpsimd.tensor_tensor(WV_lo[:], WV_raw[:], WV_hi[:].bitcast(F32), ALU.subtract).then_inc(wv_lo, 1)
                elif k == "W0":
                    w_lo(0, raw_slot(0), 0)
                elif k == "N":
                    lo(full_at[s], *views(s))
                elif k == "D":
                    if s[2] == 0:
                        w_lo(s[1] + 1, raw_slot(s[1] + 1), (s[1] + 1) % 2)
                    if s in full_at:
                        lo(full_at[s], *views(s))
                elif k in ("Y", "YS"):
                    if k == "Y" and s[1] == 0:
                        pool.wait_ge(s_out, 32)
                    lo(full_at[s], *views(s))
                elif k == "POOL":
                    for c in range(NCH):
                        lo(full_at[(*s, c)], *views((*s, c)))
                elif s == ("POOLV", 0):
                    pool.wait_ge(h_ready, LRU_T)
                    for c in range(NCH):
                        pool.wait_ge(d_free[c], u_unit(0) + 1)
                    pool_windows(nc.gpsimd, 0, link)
                    pool.wait_ge(u_kept, 1)
                    U = ST[u_unit(0) % 2]
                    for e, ((p0, p1), src) in enumerate(zip(HALVES, (PA[0], PB[0]))):
                        link(nc.gpsimd.tensor_scalar(src[p0:p1, 0:SEQ], src[p0:p1, 0:SEQ], col("inv_win", 0, 1, p0, p1), None, ALU.mult))
                        nc.gpsimd.tensor_tensor(U[p0:p1, 0:SEQ], src[p0:p1, 0:SEQ], U[p0:p1, 0:SEQ], ALU.subtract).then_inc(u_diff, 1)
                        pool.wait_ge(u_diff, e + 1)

            def clear():
                nc.gpsimd.memset(SS[:], 0.0).then_inc(ss_zero, 1)

            def units(first, g, hidden=None, piece=None, square=None, paired=None, between=None):
                parts = next_parts(paired)
                for q, (j, c, _, _) in enumerate(steps_of(paired)):
                    if q in parts:
                        v = parts[q][0]
                        w_lo(g * RAW + (first + v), (first + v + NADA) % RAW, (first + v) % 2)
                    if hidden is not None:
                        f = hidden * RAW + j
                        lo(piece + q, tile(Y_hi, f, c * CH, (c + 1) * CH),
                           tile(Y_lo, f, c * CH, (c + 1) * CH), FU[:, FF_SLOT[q], 0:CH])
                    if square is not None:
                        add_square(square + q, c, q % 2)
                    if between is not None and q >= 6:
                        between(q - 6)

            clear()
            pool.wait_ge(ss_zero, 2)
            units(N_MIX, 0, square=0)

            def lows(c, kts):
                for kt in kts:
                    lo(*norm2_piece(c, kt))

            units(N_MIX, 1, square=PER, paired=1, between=lambda k: lows(0, WOVEN[k]))
            w_lo(U_FF + 1, (U_FF + 1 + NADA) % RAW, (U_FF + 1) % 2)
            for c in range(1, NCH):
                lows(c, norm_pieces(c))
            clear()
            pool.wait_ge(ss_zero, 3)
            for g in range(KT // RAW):
                units(U_FF, g, hidden=g, piece=g * PER + P_FF, paired=0 if g == 0 else None)
            with pool.Fori(0, KT // RAW) as g:
                units(U_FF + KT, g)
            with pool.Fori(0, FF_BLOCKS - 2) as b:
                with pool.Fori(0, KT // RAW) as g:
                    units(U_MID, b * 4 + g, hidden=g, piece=b * (2 * PER) + g * PER + P_MID)
                with pool.Fori(0, KT // RAW) as g:
                    units(U_MID + KT, b * 4 + g)
            with pool.Fori(0, KT // RAW) as g:
                units(U_LAST, g, hidden=g, piece=g * PER + P_LAST)
            units(U_LAST + KT, 0, square=N_SQ)
            units(U_LAST + KT, 1, square=N_SQ + PER, paired=1)

        @block.scalar
        def _(act):
            step = Rise(act_step)

            def link(ins):
                step.off += 1
                ins.then_inc(act_step, 1)
                act.wait_ge(act_step, step.at)

            def w_hi(u, raw, s, landed, bank=NCH - 1, uses=None):
                act.wait_ge(raw_in[raw], landed)
                if not (isinstance(u, int) and u < 2):
                    act.wait_ge(d_full[bank], u - 1 if uses is None else uses)
                nc.scalar.activation(W_hi[:, s, :], RAWW[:, raw, :], ACT.Copy).then_inc(w_hi_ready, 1)

            def hi(n, hi_v, fu_v):
                act.wait_ge(full_ready, n + 1)
                nc.scalar.activation(hi_v, fu_v, ACT.Copy).then_inc(hi_ready, 1)

            def hi_key(key):
                h, _, f = views(key)
                hi(full_at[key], h, f)

            def hi_norm(n, hi_v, lo_v, fu_v, shift, kt):
                if kt >= SHIFTED:
                    hi(n, hi_v, fu_v)
                else:
                    act.wait_ge(full_ready, n + 1)
                    nc.scalar.activation(hi_v, fu_v, ACT.Identity, bias=MOD[:, shift + kt, 0:1])
                    nc.scalar.activation(fu_v, fu_v, ACT.Identity, bias=MOD[:, shift + kt, 0:1]).then_inc(hi_ready, 1)

            def root(norm, c):
                wait_full(act, norm)
                nc.scalar.activation(SS[:, c * CH:(c + 1) * CH], bank(norm)[:, 0:CH], ACT.Sqrt, bias=EPT[:], scale=1.0 / D
                                     ).then_inc(free(norm), 1)

            act.wait_ge(ld_c, 16)
            nc.scalar.activation(CTS[:], CTX[:], ACT.Sigmoid).then_inc(sig_c, 1)
            act.wait_ge(ld_cols, 16)
            link(nc.scalar.activation(LS[:, 0, :], col("lam", 0, LRU_T), ACT.Abs))
            nc.scalar.activation(LS[:, 0, :], LS[:, 0, :], ACT.Exp, scale=-1.0).then_inc(la, 1)
            act.wait_ge(lv, 1)
            nc.scalar.activation(LS[:, 2, :], LS[:, 1, :], ACT.Ln).then_inc(la, 1)
            act.wait_ge(ones_ready, 6)
            for s in plan:
                k = s[0]
                if k == "SQ":
                    c = s[1]
                    act.wait_ge(ld_x[c], 16)
                    for kt in range(KT):
                        n = c * KT + kt
                        if n >= 2:
                            act.wait_ge(ss1_done, n - 1)
                        nc.scalar.activation(SQ[:, n % 2, :], X0T[:, kt, c * CH:(c + 1) * CH], ACT.Square).then_inc(sq_ready, 1)
                elif k == "WV":
                    act.wait_ge(ld_wv, 16)
                    nc.scalar.activation(WV_hi[:], WV_raw[:], ACT.Copy).then_inc(wv_hi, 1)
                elif k == "W0":
                    w_hi(0, raw_slot(0), 0, 16 * (raw_at[("W", 0)] // RAW + 1))
                elif k == "ADA" and s[1] >= ADA_FIRST:
                    j = s[1]
                    act.wait_ge(bg_ready, 1)
                    wait_full(act, s)
                    scale = 4 * KT <= j < 5 * KT
                    nc.scalar.activation(MOD[:, j, :], bank(s)[:, 0:DEC + 1], ACT.Identity,
                                         bias=BG2[:, j - 4 * KT:j - 4 * KT + 1] if scale else col("b_ada", j),
                                         scale=col("g2", j - 4 * KT) if scale else 1.0).then_inc(free(s), 1)
                elif k == "NS":
                    root(s, s[1])
                elif k == "N":
                    hi_norm(full_at[s], *views(s), 0, s[2])
                elif k == "D":
                    _, u, c = s
                    a, b = c * CH, (c + 1) * CH
                    act.wait_ge(d_full[c], u + 1)
                    kind, t = UNIT_KIND[u]
                    src = DB[c][:, 0:CH]
                    samples = DB[c][:, LAST:CH]
                    if kind == "xr":
                        n = CH if c < NCH - 1 else LAST
                        if c == NCH - 1:
                            link(nc.scalar.activation(XS[:, t, :, CONV - 1], samples, ACT.Copy))
                        nc.scalar.activation(XR[t][:, CONV - 1 + a:CONV - 1 + a + n], DB[c][:, 0:n], ACT.Copy).then_inc(d_free[c], 1)
                    elif kind in ("k", "q", "o"):
                        n = u - 3
                        fn, scale = (ACT.Sigmoid, 1.0) if kind == "o" else (ACT.Copy, HD ** -0.5 if kind == "k" else 1.0)
                        if n >= 2 and c == 0:
                            act.wait_ge(st_stored[u % 2], 16 * st_count(u, u % 2))
                        if c == NCH - 1:
                            link(nc.scalar.activation(SG[:, n, :], samples, fn, scale=scale))
                        nc.scalar.activation(ST[u % 2][:, a:b], src, fn, scale=scale).then_inc(d_free[c], 1)
                    elif kind == "u":
                        if c == 0:
                            act.wait_ge(st_stored[u % 2], 16 * st_count(min(u, N_KQO), u % 2))
                        nc.scalar.activation(ST[u % 2][:, a:b], src, ACT.Copy).then_inc(d_free[c], 1)
                    else:
                        q = NCH * t + c
                        back = [("D", N_MIX - LRU_T + (q - 2) // NCH, (q - 2) % NCH)] if q >= 2 else [("N", NCH - 1, KT)]
                        act.wait_ge(full_ready, full_at[back[0]] + 1)
                        nc.scalar.activation(GT[:, q % 2, :], src, ACT.Gelu_apprx_tanh).then_inc(d_free[c], 1)
                        hi_key(s)
                    if c == 0:
                        seq = raw_at[("W", u + 1)]
                        w_hi(u + 1, seq % RAW, (u + 1) % 2, 16 * (seq // RAW + 1))
                    n = raw_at[("W", u)] + c + RAW
                    if n < len(raw_seq):
                        if c == 0:
                            act.wait_ge(w_lo_ready, u + 1)
                        else:
                            wait_full(act, raw_seq[n - RAW])
                        load_raw(act, n)
                elif k == "LRUG":
                    t = s[1]
                    for g, (dst, bias) in enumerate(((RG, "ba"), (IG, "bx"))):
                        for c in range(NCH):
                            key = (*s, g, c)
                            wait_full(act, key)
                            nc.scalar.activation(dst[:, c * CH:(c + 1) * CH], bank(key)[:, 0:CH], ACT.Sigmoid,
                                                 bias=col(bias, t)).then_inc(free(key), 1)
                    for c in range(NCH):
                        b, n = use[(*s, 1, c)]
                        act.wait_ge(x_free[b], n + 1)
                elif k == "LRUA":
                    t = s[1]
                    act.wait_ge(lv, 3)
                    nc.scalar.activation(TH[:], RG[:], ACT.Tanh, scale=LS[:, 5, t:t + 1]).then_inc(ah_ready, 1)
                    nc.scalar.activation(AG[:], RG[:], ACT.Exp, scale=LS[:, 4, t:t + 1]).then_inc(ah_ready, 1)
                elif k == "LRUM":
                    t = s[1]
                    act.wait_ge(m2_ready, t + 1)
                    nc.scalar.activation(MU[:], TH[:], ACT.Sqrt).then_inc(mult_ready, 1)
                elif k == "G1":
                    b, n = use[s]
                    act.wait_ge(x_free[b], n + 1)
                    link(nc.scalar.activation(GR[:, R_T, :], GR[:, R_F, :], ACT.Abs))
                    nc.scalar.activation(GR[:, R_T, :], GR[:, R_T, :], ACT.Exp, scale=-1.0).then_inc(ga, 1)
                    act.wait_ge(gv, 1)
                    nc.scalar.activation(GR[:, R_LN, :], GR[:, R_U, :], ACT.Ln).then_inc(ga, 1)
                elif k == "G3":
                    act.wait_ge(nm_ready, 1)
                    nc.scalar.activation(GR[:, R_INT, :], GR[:, R_M, :], ACT.Exp, bias=MPC[:], scale=-1.0).then_inc(int_ready, 1)
                    nc.scalar.activation(GR[:, R_W, :], GR[:, R_A, :], ACT.Exp, bias=GR[:, R_NM, LC - 1:LC]).then_inc(ga, 1)
                    act.wait_ge(gv, 4)
                    nc.scalar.activation(GR[:, R_EM, :], GR[:, R_EM, :], ACT.Exp, scale=-1.0).then_inc(ga, 1)
                elif k == "S":
                    act.wait_ge(ex_ready, s[1] + 1)
                    nc.scalar.activation(EX[:], EX[:], ACT.Exp).then_inc(ex_exp, 1)
                elif k == "AB":
                    act.wait_ge(z_ready, s[1] + 1)
                    nc.scalar.activation(SM4[:, 5, :], SM4[:, 4, :], ACT.Sqrt, bias=EPT[:], scale=1.0 / HD).then_inc(z_root, 1)
                elif k in ("Y", "YS"):
                    hi_key(s)
                elif k == "POOL":
                    for c in range(NCH):
                        hi_key((*s, c))
                elif k == "SMA":
                    act.wait_ge(sma_t, 1)
                    nc.scalar.activation(SR[:, :, 0:2], SR[:, :, 0:2], ACT.Exp).then_inc(sma_e, 1)
                    nc.scalar.activation(SR[:, :, 2], SR[:, :, 3], ACT.Exp, scale=-1.0).then_inc(sma_e, 1)
                elif k == "SMC":
                    act.wait_ge(smc_z, 1)
                    nc.scalar.activation(D32[:, 5:6], D32[:, 4:5], ACT.Sqrt, bias=EPT[0:DEC * HEADS, :], scale=1.0 / HD).then_inc(smc_root, 1)

            def units(first, g, hidden=None, piece=None, square=None, paired=None, between=None):
                parts = next_parts(paired)
                for q, (j, c, bank, v) in enumerate(steps_of(paired)):
                    if q in parts:
                        w, last, use_of = parts[q]
                        w_hi(g * RAW + (first + w), (first + w + NADA) % RAW, (first + w) % 2,
                             g * 16 + 16 * ((first + w + NADA) // RAW + 1), last, g * RAW + (first + use_of + 1))
                    n = g * RAW + (first + v + 1)
                    if hidden is not None:
                        act.wait_ge(d_full[bank], n)
                        act.wait_ge(full_ready, piece + (q - 1))
                        nc.scalar.activation(GT[:, q % 2, :], DB[bank][:, 0:CH], ACT.Relu).then_inc(d_free[bank], 1)
                        hi(piece + q, tile(Y_hi, hidden * RAW + j, c * CH, (c + 1) * CH), FU[:, FF_SLOT[q], 0:CH])
                    if square is not None:
                        act.wait_ge(d_free[bank], n)
                        if square + q >= 2:
                            act.wait_ge(ss_done, square + (q - 1))
                        nc.scalar.activation(SQ[:, q % 2, :], tile(X, g * RAW + j, c * CH, (c + 1) * CH), ACT.Square).then_inc(sq_ready, 1)
                    if between is not None and q >= 6:
                        between(q - 6)

            units(N_MIX, 0, square=0)

            mod_ready(act)

            def roots(n, k):
                for c in {2: (0,), 4: (1,), 5: (2,)}.get(k, ()):
                    root(("NORM", n, c), c)

            def highs(c, kts):
                for kt in kts:
                    hi_norm(*norm2_piece(c, kt), 3 * KT, kt)

            def after_out(k):
                if k < 5:
                    roots(2, k)
                highs(0, WOVEN[k])

            units(N_MIX, 1, square=PER, paired=1, between=after_out)
            u = U_FF + 1
            w_hi(u, (u + NADA) % RAW, u % 2, 16 * ((u + NADA) // RAW + 1))
            root(("NORM", 2, 2), 2)
            for c in range(1, NCH):
                highs(c, norm_pieces(c))
            for g in range(KT // RAW):
                units(U_FF, g, hidden=g, piece=g * PER + P_FF, paired=0 if g == 0 else None)
            with act.Fori(0, KT // RAW) as g:
                units(U_FF + KT, g)
            with act.Fori(0, FF_BLOCKS - 2) as b:
                with act.Fori(0, KT // RAW) as g:
                    units(U_MID, b * 4 + g, hidden=g, piece=b * (2 * PER) + g * PER + P_MID)
                with act.Fori(0, KT // RAW) as g:
                    units(U_MID + KT, b * 4 + g)
            with act.Fori(0, KT // RAW) as g:
                units(U_LAST, g, hidden=g, piece=g * PER + P_LAST)
            units(U_LAST + KT, 0, square=N_SQ)
            units(U_LAST + KT, 1, square=N_SQ + PER, paired=1, between=lambda k: roots(3, k))

        @block.vector
        def _(dve):
            step = Rise(dve_step)
            V = nc.vector

            def link(ins):
                step.off += 1
                ins.then_inc(dve_step, 1)
                dve.wait_ge(dve_step, step.at)

            def tell(ins, s, n):
                ins.then_inc(s, 1)
                dve.wait_ge(s, n)

            def slot_free(n):
                if not (isinstance(n, int) and n < FUS):
                    dve.wait_ge(lo_ready, n - (FUS - 1))
                return (n % FUS) if isinstance(n, int) else None

            def put_free(ins, key):
                tell(ins, free(key), use[key][1] + 1)

            for ins in (V.memset(ONE[:], 1.0), V.memset(EPT[:], EPS), V.memset(GTE[:], 0.0), V.memset(MP[:], 0.0),
                        V.memset(VS[0][:, :, HD:HV], 1.0), V.memset(VS[1][:, :, HD:HV], 1.0)):
                ins.then_inc(ones_ready, 1)
            dve.wait_ge(ones_ready, 6)
            dve.wait_ge(sig_c, 1)
            tell(V.tensor_tensor(CTX[:], CTX[:], CTS[:], ALU.mult), c_ready, 1)
            dve.wait_ge(ld_cols, 16)

            def ada(j):
                wait_full(dve, ("ADA", j))
                put_free(V.tensor_scalar(MOD[:, j, :], bank(("ADA", j))[:, 0:DEC + 1], col("b_ada", j), None, ALU.add), ("ADA", j))
                if j >= KT:
                    link(V.tensor_scalar(MOD[:, j, :], MOD[:, j, :], 1.0, col("g1", j - KT), ALU.add, ALU.mult))

            def normed(x, c, kt, n, shift, scale):
                f = slot_free(n)
                if kt < KT:
                    _, _, a, w = norm_target(c, kt)
                    one = V.scalar_tensor_tensor(out=FU[:, f, 0:w], in0=x[:, kt, a:a + w], scalar=MOD[:, scale + kt, 0:1],
                                                 in1=SS[:, a:a + w], op0=ALU.mult, op1=ALU.mult)
                    if kt >= SHIFTED:
                        link(one)
                        one = V.tensor_scalar(FU[:, f, 0:w], FU[:, f, 0:w], MOD[:, shift + kt, 0:1], None, ALU.add)
                    one.then_inc(full_ready, 1)
                else:
                    v = FU[:, f, 0:KT * DEC].rearrange("p (k b) -> p k b", k=KT)
                    link(V.tensor_tensor(v, x[:, :, SEQ:], over(SS[:, SEQ:], KT), ALU.mult))
                    link(V.tensor_tensor(v, v, MOD[:, scale:scale + KT, 1:], ALU.mult))
                    V.tensor_tensor(v, v, MOD[:, shift:shift + KT, 1:], ALU.add).then_inc(full_ready, 1)

            def inverse_root(norm, c):
                b, n = use[norm]
                dve.wait_ge(x_free[b], n + 1)
                link(V.reciprocal(SS[:, c * CH:(c + 1) * CH], SS[:, c * CH:(c + 1) * CH]))

            link(V.tensor_scalar(BG2[:], col("b_ada", 4 * KT, KT), 1.0, None, ALU.add))
            V.tensor_tensor(BG2[:], BG2[:], col("g2", 0, KT), ALU.mult).then_inc(bg_ready, 1)

            dve.wait_ge(la, 1)
            tell(V.tensor_scalar(LS[:, 1, :], LS[:, 0, :], 1.0, None, ALU.add), lv, 1)
            link(V.tensor_scalar(LS[:, 3, :], LS[:, 1, :], -1.0, None, ALU.add))
            link(V.tensor_tensor(LS[:, 3, :], LS[:, 0, :], LS[:, 3, :], ALU.subtract))
            link(V.reciprocal(LS[:, 4, :], LS[:, 1, :]))
            link(V.tensor_tensor(LS[:, 3, :], LS[:, 3, :], LS[:, 4, :], ALU.mult))
            dve.wait_ge(la, 2)
            link(V.tensor_tensor(LS[:, 3, :], LS[:, 3, :], LS[:, 2, :], ALU.add))
            link(V.tensor_scalar(LS[:, 0, :], col("lam", 0, LRU_T), 0.0, None, ALU.min))
            link(V.tensor_tensor(LS[:, 0, :], LS[:, 0, :], LS[:, 3, :], ALU.subtract))
            tell(V.tensor_scalar(LS[:, 4, :], LS[:, 0, :], 8.0, None, ALU.mult), lv, 2)
            tell(V.tensor_scalar(LS[:, 5, :], LS[:, 0, :], -8.0, None, ALU.mult), lv, 3)
            for s in plan:
                k = s[0]
                if k == "SQ":
                    c = s[1]
                    dve.wait_ge(ss_zero, 1)
                    for n in range(c * KT, (c + 1) * KT):
                        dve.wait_ge(sq_ready, n + 1)
                        tell(V.tensor_tensor(SS[:, c * CH:(c + 1) * CH], SS[:, c * CH:(c + 1) * CH], SQ[:, n % 2, :], ALU.add),
                             ss1_done, n + 1)
                elif k == "NS":
                    inverse_root(s, s[1])
                elif k == "N":
                    normed(X0T, s[1], s[2], full_at[s], 0, KT)
                elif k == "ADA" and s[1] < ADA_FIRST:
                    ada(s[1])
                elif k == "V":
                    t = s[1]
                    wait_full(dve, s)
                    ps = bank(s)
                    if t < NLC:
                        if t >= 2:
                            dve.wait_ge(v_stored[t % 2], 16 * (t // 2))
                        tell(V.tensor_copy(VS[t % 2][:, :, 0:HD], heads(ps[:, 0:HEADS * HD])), v_ready, t + 1)
                        put_free(V.tensor_copy(GTE[:, :, t], ps[:, HEADS * HD:VCOLS]), s)
                    else:
                        tell(V.tensor_copy(VS8[:], ps[0:DEC, 0:HEADS * HD]), v8_ready, 1)
                        put_free(V.tensor_copy(GTE[0:DEC, :, t], ps[0:DEC, HEADS * HD:VCOLS]), s)
                elif k == "G1":
                    dve.wait_ge(ld_small, 16 * 6)
                    wait_full(dve, s)
                    ps = bank(s)
                    link(V.tensor_scalar(GR[:, R_I, :], ps[0:ROWS, 0:LC], GB[:, 0:1], None, ALU.add))
                    put_free(V.tensor_scalar(GR[:, R_F, :], ps[0:ROWS, LC:2 * LC], GB[:, 1:2], None, ALU.add), s)
                    dve.wait_ge(ga, 1)
                    tell(V.tensor_scalar(GR[:, R_U, :], GR[:, R_T, :], 1.0, None, ALU.add), gv, 1)
                    link(V.tensor_scalar(GR[:, R_C, :], GR[:, R_U, :], -1.0, None, ALU.add))
                    link(V.tensor_tensor(GR[:, R_C, :], GR[:, R_T, :], GR[:, R_C, :], ALU.subtract))
                    link(V.reciprocal(GR[:, R_LF, :], GR[:, R_U, :]))
                    link(V.tensor_tensor(GR[:, R_C, :], GR[:, R_C, :], GR[:, R_LF, :], ALU.mult))
                    dve.wait_ge(ga, 2)
                    link(V.tensor_tensor(GR[:, R_C, :], GR[:, R_C, :], GR[:, R_LN, :], ALU.add))
                    link(V.tensor_scalar(GR[:, R_T, :], GR[:, R_F, :], 0.0, None, ALU.min))
                    link(V.tensor_tensor(GR[:, R_LF, :], GR[:, R_T, :], GR[:, R_C, :], ALU.subtract))
                    link(V.tensor_tensor_scan(GR[:, R_BC, :], ONE[0:ROWS, :], GR[:, R_LF, :], 0.0, ALU.mult, ALU.add))
                    link(V.tensor_tensor(GR[:, R_A, :], GR[:, R_I, :], GR[:, R_BC, :], ALU.subtract))
                    tell(V.tensor_tensor_scan(GR[:, R_M, :], GR[:, R_A, :], GR[:, R_A, :], NEG_BIG, ALU.max, ALU.max), gv, 2)
                elif k == "G2":
                    wait_full(dve, s)
                    put_free(V.tensor_copy(BM[:], bank(s)[0:1, 0:2 * ROWS]), s)
                    for h in range(HEADS):
                        r = h * (NLC + 1)
                        one = V.tensor_tensor_scan(MP[:, r + 1:r + 1 + NLC], BM[:, ROWS + r:ROWS + r + NLC], BM[:, r:r + NLC],
                                                   0.0, ALU.max, ALU.add)
                        if h < HEADS - 1:
                            link(one)
                    tell(one, gv, 3)
                elif k == "G3":
                    wait_full(dve, s)
                    put_free(V.tensor_copy(MPC[:], bank(s)[0:ROWS, 0:1]), s)
                    link(V.tensor_scalar(GR[:, R_M, :], GR[:, R_M, :], MPC[:], None, ALU.max))
                    tell(V.tensor_scalar(GR[:, R_NM, :], GR[:, R_M, :], -1.0, None, ALU.mult), nm_ready, 1)
                    tell(V.tensor_tensor(GR[:, R_EM, :], GR[:, R_BC, :], GR[:, R_M, :], ALU.add), gv, 4)
                elif k == "G4":
                    wait_full(dve, s)
                    put_free(V.tensor_copy(COL[:].rearrange("p k r -> p (k r)"), bank(s)[:, 0:4 * ROWS]), s)
                elif k == "LRUC":
                    t = s[1]
                    link(V.memset(XR[t][:, 0:CONV - 1], 0.0))
                    for c in range(NCH):
                        dve.wait_ge(d_free[c], t + 1)
                    w = lambda j: col("conv_w", t * CONV + j)
                    link(V.tensor_scalar(XC[:, 0:SEQ], XR[t][:, CONV - 1:], w(CONV - 1), col("conv_b", t), ALU.mult, ALU.add))
                    link(V.tensor_scalar(XC[:, SEQ:], XS[:, t, :, CONV - 1], w(CONV - 1), col("conv_b", t), ALU.mult, ALU.add))
                    for j in range(CONV - 1):
                        link(V.scalar_tensor_tensor(out=XC[:, 0:SEQ], in0=XR[t][:, j:j + SEQ], scalar=w(j), in1=XC[:, 0:SEQ],
                                                    op0=ALU.mult, op1=ALU.add))
                        link(V.scalar_tensor_tensor(out=XC[:, SEQ:], in0=XS[:, t, :, j], scalar=w(j), in1=XC[:, SEQ:],
                                                    op0=ALU.mult, op1=ALU.add))
                    tell(V.tensor_copy(OUTC[:, t, :], XR[t][:, SEQ:]), xc_ready, t + 1)
                elif k == "LRUA":
                    t = s[1]
                    dve.wait_ge(ah_ready, 2 * (t + 1))
                    link(V.tensor_tensor(MU[:], AG[:], AG[:], ALU.mult))
                    tell(V.scalar_tensor_tensor(out=TH[:], in0=MU[:], scalar=1.0, in1=TH[:], op0=ALU.add, op1=ALU.mult),
                         m2_ready, t + 1)
                    link(V.tensor_tensor(BT[:], IG[:], XC[:], ALU.mult))
                elif k == "LRUM":
                    t = s[1]
                    dve.wait_ge(mult_ready, t + 1)
                    link(V.memset(MU[:, 0:1], 1.0))
                    link(V.tensor_tensor(BT[:], BT[:], MU[:], ALU.mult))
                    link(V.tensor_tensor_scan(HS[t][:, 0:SEQ], AG[:, 0:SEQ], BT[:, 0:SEQ], 0.0, ALU.mult, ALU.add))
                    link(V.tensor_tensor(T8[:], AG[:, SEQ:], col("h0", t * DEC, DEC), ALU.mult))
                    link(V.tensor_tensor(HS[t][:, SEQ:], T8[:], BT[:, SEQ:], ALU.add))
                    tell(V.tensor_copy(OUTL[:, t, :], HS[t][:, SEQ - 1:]), h_ready, t + 1)
                elif k == "D" and UNIT_KIND[s[1]][0] == "gr":
                    _, u, c = s
                    t, n = UNIT_KIND[u][1], full_at[s]
                    dve.wait_ge(d_free[c], u + 1)
                    f = slot_free(n)
                    tell(V.tensor_tensor(FU[:, f, 0:CH], GT[:, (NCH * t + c) % 2, :], HS[t][:, c * CH:(c + 1) * CH], ALU.mult),
                         full_ready, n + 1)
                elif k == "TS":
                    for w in range(2):
                        wait_full(dve, ("TS", w))
                        put_free(V.tensor_copy(QK8[:, w, :], bank(("TS", w))[0:DEC, 0:HEADS * HD]), ("TS", w))
                elif k == "S":
                    c = s[1]
                    dve.wait_ge(ld_kqv[c % 2], 16 * 3 * (c // 2 + 1))
                    if c == 0:
                        tell(V.memset(CN[:], 0.0), cn_ready, 1)
                        dve.wait_ge(ld_dec, 16)
                        dve.wait_ge(ld_mask, 16)
                    dve.wait_ge(ld_nm, 16 * (c + 1))
                    link(V.tensor_tensor(EX[:], NM[:], wide(colh(0, c), LC), ALU.add))
                    tell(V.tensor_tensor(EX[:], EX[:], over(MASK[:], HEADS), ALU.min), ex_ready, c + 1)
                    wait_full(dve, ("KT", c))
                    put_free(V.tensor_tensor(KW[:], heads(bank(("KT", c))[:, 0:HEADS * HD]), wide(colh(1, c), HD), ALU.mult), ("KT", c))
                    dve.wait_ge(ex_exp, c + 1)
                    wait_full(dve, s)
                    put_free(V.tensor_tensor(EX[:], bank(s)[:, 0:HEADS * LC].rearrange("p (h t) -> p h t", h=HEADS), EX[:], ALU.mult), s)
                elif k == "AB":
                    c = s[1]
                    A, B = ("A", c), ("B", c)
                    wait_full(dve, B)
                    put_free(V.tensor_tensor(T1[:], bank(B)[:, 0:HEADS * HV].rearrange("p (h v) -> p h v", h=HEADS),
                                             wide(colh(2, c), HV), ALU.mult), B)
                    wait_full(dve, A)
                    put_free(V.tensor_tensor(NUM[:], bank(A)[:, 0:HEADS * HV].rearrange("p (h v) -> p h v", h=HEADS), T1[:], ALU.add), A)
                    den = NUM[:, :, HD]
                    link(V.scalar_tensor_tensor(out=SM4[:, 0, :], in0=den, scalar=-1.0, in1=den, op0=ALU.mult, op1=ALU.max))
                    link(V.tensor_tensor(SM4[:, 1, :], SM4[:, 0, :], colh(3, c), ALU.max))
                    link(V.reciprocal(SM4[:, 2, :], SM4[:, 1, :]))
                    if c >= 4:
                        dve.wait_ge(x_full["X3"], use[("Y", c - 4)][1] + 1)
                    link(V.tensor_tensor(HM[c % 4][:], NUM[:, :, 0:HD], wide(SM4[:, 2, :], HD), ALU.mult))
                    link(V.tensor_tensor(T1[:, :, 0:HD], HM[c % 4][:], HM[c % 4][:], ALU.mult))
                    tell(V.tensor_reduce(SM4[:, 4, :], T1[:, :, 0:HD], AX_X, ALU.add), z_ready, c + 1)
                    dve.wait_ge(z_root, c + 1)
                    link(V.reciprocal(SM4[:, 6, :], SM4[:, 5, :]))
                    tell(V.tensor_tensor(HM[c % 4][:], HM[c % 4][:], wide(SM4[:, 6, :], HD), ALU.mult), hm_ready, c + 1)
                elif k == "U":
                    c = s[1]
                    link(V.tensor_tensor(CN[:], CN[:], wide(DECB[:].rearrange("p (h c) -> p h c", c=NLC + 1)[:, :, c], HV), ALU.mult))
                    wait_full(dve, s)
                    put_free(V.tensor_tensor(CN[:], bank(s)[0:HD, 0:HEADS * HV].rearrange("p (h v) -> p h v", h=HEADS), CN[:], ALU.add), s)
                elif k in ("Y", "YS"):
                    n = full_at[s]
                    f = slot_free(n)
                    wait_full(dve, s)
                    if k == "Y":
                        dve.wait_ge(ld_o, 16 * (s[1] + 1))
                    w = LC if k == "Y" else DEC
                    for j in range(ML_T):
                        o = OT[:, j, :] if k == "Y" else SG[:, 2 * ML_T + j, :]
                        one = V.scalar_tensor_tensor(out=FU[:, f, j * w:(j + 1) * w], in0=bank(s)[:, j * w:(j + 1) * w],
                                                     scalar=col("ml_g", j), in1=o, op0=ALU.mult, op1=ALU.mult)
                        if j < ML_T - 1:
                            link(one)
                    tell(one, full_ready, n + 1)
                    dve.sem_inc(free(s), 1)
                elif k == "POOLV":
                    j = s[1]
                    u = N_MIX - LRU_T - POOL_T + j
                    for c in range(NCH):
                        dve.wait_ge(d_free[c], u + 1)
                    U = ST[u % 2]
                    tell(V.tensor_copy(UO[:, j, :], U[:, SEQ - PBUF:SEQ]), u_kept, j + 1)
                    link(V.tensor_copy(UB[:, j, :, PBUF], U[:, SEQ:]))
                    for (p0, p1), win in zip(HALVES, WINS[2 * j:2 * j + 2]):
                        link(V.tensor_reduce(UM[p0:p1, :], UB[p0:p1, j, :, PBUF + 1 - win:], AX_X, ALU.add))
                        one = V.scalar_tensor_tensor(out=U[p0:p1, SEQ:], in0=UM[p0:p1, :], scalar=col("inv_win", j, 1, p0, p1),
                                                     in1=U[p0:p1, SEQ:], op0=ALU.mult, op1=ALU.subtract)
                        if p0 == 0:
                            link(one)
                        else:
                            tell(one, u_small, j + 1)
                    if j == 1:
                        pool_windows(V, 1, link)
                elif k == "POOLD":
                    U = ST[u_unit(1) % 2]
                    for e, ((p0, p1), src) in enumerate(zip(HALVES, (PA[1], PB[1]))):
                        tell(V.scalar_tensor_tensor(out=U[p0:p1, 0:SEQ], in0=src[p0:p1, 0:SEQ], scalar=col("inv_win", 1, 1, p0, p1),
                                                    in1=U[p0:p1, 0:SEQ], op0=ALU.mult, op1=ALU.subtract), u1_diff, e + 1)
                elif k == "POOL":
                    j = s[1]
                    for c in range(NCH):
                        n = full_at[(*s, c)]
                        f = slot_free(n)
                        wait_full(dve, (*s, c))
                        tell(V.tensor_scalar(FU[:, f, 0:CH], bank((*s, c))[:, 0:CH], col("pool_scale", j), None, ALU.mult),
                             full_ready, n + 1)
                        dve.sem_inc(free((*s, c)), 1)
                elif k == "SMA":
                    link(V.tensor_tensor(SR[:, :, 1], GR[:, R_LF, 0:DEC], M0[:], ALU.add))
                    link(V.tensor_tensor(SR[:, :, 3], SR[:, :, 1], GR[:, R_I, 0:DEC], ALU.max))
                    link(V.tensor_tensor(SR[:, :, 1], SR[:, :, 1], SR[:, :, 3], ALU.subtract))
                    tell(V.tensor_tensor(SR[:, :, 0], GR[:, R_I, 0:DEC], SR[:, :, 3], ALU.subtract), sma_t, 1)
                elif k == "SMB":
                    if s[1] == 0:
                        dve.wait_ge(ld_st, 32)
                        dve.wait_ge(ld_s, 16 * N_LD_S)
                        link(V.tensor_scalar(K32[:], K32[:], S32[:, 0:1], None, ALU.mult))
                        link(V.scalar_tensor_tensor(out=N32[:], in0=N32[:], scalar=S32[:, 1:2], in1=K32[:], op0=ALU.mult, op1=ALU.add))
                        link(V.tensor_tensor(T32[:], N32[:], Q32[:], ALU.mult))
                        link(V.tensor_reduce(D32[:, 0:1], T32[:], AX_X, ALU.add))
                        link(V.tensor_scalar(K128[:], K128[:], S128[:, 0:1], None, ALU.mult))
                    VQ = VH // 4
                    a, b = s[1] * VQ, (s[1] + 1) * VQ
                    link(V.tensor_tensor(TC[:], wide(V24[:, a:b], HD), over(K128[:], VQ), ALU.mult))
                    link(V.scalar_tensor_tensor(out=CS[:, a:b, :], in0=CS[:, a:b, :], scalar=S128[:, 1:2], in1=TC[:],
                                                op0=ALU.mult, op1=ALU.add))
                    link(V.tensor_tensor(TC[:], CS[:, a:b, :], over(Q128[:], VQ), ALU.mult))
                    one = V.tensor_reduce(H24[:, a:b], TC[:], AX_X, ALU.add)
                    if s[1] < 3:
                        link(one)
                    else:
                        tell(one, smb_h, 1)
                elif k == "SMC":
                    dve.wait_ge(ld_h32, 16)
                    link(V.scalar_tensor_tensor(out=D32[:, 1:2], in0=D32[:, 0:1], scalar=-1.0, in1=D32[:, 0:1], op0=ALU.mult, op1=ALU.max))
                    link(V.tensor_tensor(D32[:, 2:3], D32[:, 1:2], S32[:, 2:3], ALU.max))
                    link(V.reciprocal(D32[:, 3:4], D32[:, 2:3]))
                    link(V.tensor_scalar(H32[:], H32[:], D32[:, 3:4], None, ALU.mult))
                    link(V.tensor_tensor(T32[:], H32[:], H32[:], ALU.mult))
                    tell(V.tensor_reduce(D32[:, 4:5], T32[:], AX_X, ALU.add), smc_z, 1)
                    dve.wait_ge(smc_root, 1)
                    link(V.reciprocal(D32[:, 6:7], D32[:, 5:6]))
                    tell(V.tensor_scalar(H32[:], H32[:], D32[:, 6:7], None, ALU.mult), smc_y, 1)

            def units(first, g, residual=None, hidden=None, piece=None, paired=None, between=None):
                for q, (j, c, bank, v) in enumerate(steps_of(paired)):
                    a, n = c * CH, g * RAW + (first + v + 1)
                    if hidden is not None:
                        dve.wait_ge(d_free[bank], n)
                        slot_free(piece + q)
                        V.tensor_tensor(FU[:, FF_SLOT[q], 0:CH], GT[:, q % 2, :], GT[:, q % 2, :], ALU.mult).then_inc(full_ready, 1)
                        continue
                    gate, tiles = residual
                    m_x, m_g = tiles * RAW + j, tiles * RAW + (gate + j)
                    dve.wait_ge(d_full[bank], n)
                    w = CH
                    if c == NCH - 1:
                        w = LAST
                        link(V.tensor_tensor(T8[:], DB[bank][:, LAST:CH], tile(MOD, m_g, 1, DEC + 1), ALU.mult))
                        link(V.tensor_tensor(tile(X, m_x, SEQ, TOK), tile(X, m_x, SEQ, TOK), T8[:], ALU.add))
                    tell(V.scalar_tensor_tensor(out=tile(X, m_x, a, a + w), in0=DB[bank][:, 0:w], scalar=tile(MOD, m_g, 0, 1),
                                                in1=tile(X, m_x, a, a + w), op0=ALU.mult, op1=ALU.add), d_free[bank], n)
                    if between is not None and q >= 6:
                        between(q - 6)

            mod_ready(dve)

            def pieces2(c, kts):
                for kt in kts:
                    normed(X, c, kt, P_MIX + c * KT + kt, 3 * KT, 4 * KT)

            def after_out(k):
                if k == 2:
                    inverse_root(("NORM", 2, 0), 0)
                pieces2(0, WOVEN[k])

            for g in range(N_OUT // RAW):
                for m in range(g * RAW, (g + 1) * RAW):
                    dve.wait_ge(ld_xres[m], 16)
                units(N_MIX, g, residual=(2 * KT, g), paired=1 if g else None, between=after_out if g else None)
            for c in range(1, NCH):
                inverse_root(("NORM", 2, c), c)
                pieces2(c, norm_pieces(c))
            for g in range(KT // RAW):
                units(U_FF, g, hidden=g, piece=g * PER + P_FF, paired=0 if g == 0 else None)
            with dve.Fori(0, KT // RAW) as g:
                step.enter(g, 2 * RAW)
                units(U_FF + KT, g, residual=(5 * KT, g))
                step.leave(KT // RAW)
            before = step.at
            with dve.Fori(0, FF_BLOCKS - 2) as b:
                with dve.Fori(0, KT // RAW) as g:
                    units(U_MID, b * 4 + g, hidden=g, piece=b * (2 * PER) + g * PER + P_MID)
                with dve.Fori(0, KT // RAW) as g:
                    step.base, step.off = b * (4 * RAW) + g * (2 * RAW) + before, 0
                    units(U_MID + KT, b * 4 + g, residual=(5 * KT, g))
                    assert step.off == 2 * RAW
            step.base, step.off = before + (FF_BLOCKS - 2) * 4 * RAW, 0
            with dve.Fori(0, KT // RAW) as g:
                units(U_LAST, g, hidden=g, piece=g * PER + P_LAST)
            units(U_LAST + KT, 0, residual=(5 * KT, 0))

            def final(c, kts):
                for kt in kts:
                    a, b = c * CH, (c + 1) * CH
                    V.scalar_tensor_tensor(out=OUTN[:, kt, a:b], in0=X[:, kt, a:b], scalar=col("gf", kt), in1=SS[:, a:b],
                                           op0=ALU.mult, op1=ALU.mult).then_inc(fin_ready, 1)

            def after_last(k):
                if k == 2:
                    inverse_root(("NORM", 3, 0), 0)
                final(0, WOVEN[k])

            units(U_LAST + KT, 1, residual=(5 * KT, 1), paired=1, between=after_last)
            for c in range(1, NCH):
                inverse_root(("NORM", 3, c), c)
                final(c, range(KT))

        @block.tensor
        def _(pe):
            T = nc.tensor

            def take(key):
                b, n = use[key]
                if n:
                    pe.wait_ge(x_free[b], n)
                return XB[b]

            def done(ins, key):
                ins.then_inc(x_full[use[key][0]], 1)

            def ada(j):
                raw = raw_wait(pe, ("ADA", j))
                ps = take(("ADA", j))
                for kt in range(KT):
                    one = T.matmul(ps[:, 0:DEC + 1], RAWW[:, raw, kt * P:(kt + 1) * P], CTX[:, kt, :], start=(kt == 0), stop=(kt == KT - 1))
                done(one, ("ADA", j))

            def sum_squares(key, c, added, upto):
                pe.wait_ge(added, upto)
                ps = take(key)
                done(T.matmul(ps[:, 0:CH], ONE[:], SS[:, c * CH:(c + 1) * CH], start=True, stop=True), key)

            def dense(s, c, hi, lo, bank):
                for kt in range(KT):
                    w_h, w_l = W_hi[:, s, kt * P:(kt + 1) * P], W_lo[:, s, kt * P:(kt + 1) * P]
                    a, b = c * CH, (c + 1) * CH
                    T.matmul(DB[bank][:, 0:CH], w_h, hi[:, kt, a:b], start=(kt == 0), stop=False)
                    T.matmul(DB[bank][:, 0:CH], w_h, lo[:, kt, a:b], start=False, stop=False)
                    one = T.matmul(DB[bank][:, 0:CH], w_l, hi[:, kt, a:b], start=False, stop=(kt == KT - 1))
                one.then_inc(d_full[bank], 1)

            pe.wait_ge(c_ready, 1)
            pe.wait_ge(ones_ready, 6)
            for s in plan:
                k = s[0]
                if k == "NS":
                    sum_squares(s, s[1], ss1_done, (s[1] + 1) * KT)
                elif k == "ADA":
                    ada(s[1])
                elif k == "V":
                    t = s[1]
                    a = t * LC
                    m = min(LC, TOK - a)
                    pe.wait_ge(wv_lo, 1)
                    pe.wait_ge(lo_ready, norm_done((a + m - 1) // CH))
                    ps = take(s)
                    for kt in range(KT):
                        h, l = H_hi[:, kt, a:a + m], H_lo[:, kt, a:a + m]
                        T.matmul(ps[0:m, 0:VCOLS], h, WV_hi[:, kt, :], start=(kt == 0), stop=False)
                        T.matmul(ps[0:m, 0:VCOLS], h, WV_lo[:, kt, :], start=False, stop=False)
                        one = T.matmul(ps[0:m, 0:VCOLS], l, WV_hi[:, kt, :], start=False, stop=(kt == KT - 1))
                    done(one, s)
                elif k == "D":
                    _, u, c = s
                    pe.wait_ge(w_lo_ready, u + 1)
                    if u:
                        pe.wait_ge(d_free[c], u)
                    dense(u % 2, c, H_hi, H_lo, c)
                elif k == "G1":
                    b, n = use[("V", NLC)]
                    pe.wait_ge(x_free[b], n + 1)
                    pe.wait_ge(ld_small, 16 * 6)
                    ps = take(s)
                    T.transpose(ps[0:ROWS, 0:LC], GTE[:, 0:HEADS, :].rearrange("p g c -> p (g c)"), IDN[:])
                    done(T.transpose(ps[0:ROWS, LC:2 * LC], GTE[:, HEADS:, :].rearrange("p g c -> p (g c)"), IDN[:]), s)
                elif k == "G2":
                    pe.wait_ge(gv, 2)
                    ps = take(s)
                    T.matmul(ps[0:1, 0:ROWS], GR[:, R_BC, LC - 1:LC], IDN[0:ROWS, 0:ROWS], start=True, stop=True)
                    done(T.matmul(ps[0:1, ROWS:2 * ROWS], GR[:, R_M, LC - 1:LC], IDN[0:ROWS, 0:ROWS], start=True, stop=True), s)
                elif k == "G3":
                    pe.wait_ge(gv, 3)
                    done(T.matmul(take(s)[0:ROWS, 0:1], MP[:], ONE[0:1, 0:1], start=True, stop=True), s)
                elif k == "G4":
                    pe.wait_ge(ga, 4)
                    pe.wait_ge(int_ready, 1)
                    ps = take(s)
                    for i, r in enumerate((R_A, R_W, R_INT, R_EM)):
                        one = T.transpose(ps[:, i * ROWS:(i + 1) * ROWS], GR[:, r, :], IDN[0:ROWS, 0:ROWS])
                    done(one, s)
                elif k == "LRUG":
                    t = s[1]
                    pe.wait_ge(xc_ready, t + 1)
                    pe.wait_ge(ld_bdl, 16)
                    for g in range(2):
                        for c in range(NCH):
                            key = (*s, g, c)
                            done(T.matmul(take(key)[:, 0:CH], BDL[:, g * LRU_T + t, :], XC[:, c * CH:(c + 1) * CH], start=True, stop=True), key)
                elif k == "TS":
                    pe.wait_ge(d_free[NCH - 1], 3 + 2 * ML_T)
                    for w in range(2):
                        ps = take(("TS", w))
                        for j in range(ML_T):
                            one = T.transpose(ps[0:DEC, j * P:(j + 1) * P], SG[:, w * ML_T + j, :], IDN[:])
                        done(one, ("TS", w))
                elif k == "S":
                    c = s[1]
                    b = c % 2
                    pe.wait_ge(ld_kqv[b], 16 * 3 * (c // 2 + 1))
                    ps = take(("KT", c))
                    for h in range(HEADS):
                        one = T.transpose(ps[:, h * HD:(h + 1) * HD], K96[b][:, h, :], IDN[0:HD, 0:HD])
                    done(one, ("KT", c))
                    ps = take(s)
                    for h in range(HEADS):
                        one = T.matmul(ps[:, h * LC:(h + 1) * LC], K96[b][:, h, :], Q96[b][:, h, :], start=True, stop=True)
                    done(one, s)
                elif k == "AB":
                    c = s[1]
                    b = c % 2
                    if c == 0:
                        pe.wait_ge(cn_ready, 1)
                    else:
                        bk, n = use[("U", c - 1)]
                        pe.wait_ge(x_free[bk], n + 1)
                    ps = take(("B", c))
                    for h in range(HEADS):
                        one = T.matmul(ps[:, h * HV:(h + 1) * HV], Q96[b][:, h, :], CN[:, h, :], start=True, stop=True)
                    done(one, ("B", c))
                    bk, n = use[("S", c)]
                    pe.wait_ge(x_free[bk], n + 1)
                    ps = take(("A", c))
                    for h in range(HEADS):
                        one = T.matmul(ps[:, h * HV:(h + 1) * HV], EX[:, h, :], VB[b][:, h, :], start=True, stop=True)
                    done(one, ("A", c))
                elif k == "U":
                    c = s[1]
                    bk, n = use[("KT", c)]
                    pe.wait_ge(x_free[bk], n + 1)
                    ps = take(s)
                    for h in range(HEADS):
                        one = T.matmul(ps[0:HD, h * HV:(h + 1) * HV], KW[:, h, :], VB[c % 2][:, h, :], start=True, stop=True)
                    done(one, s)
                elif k == "Y":
                    c = s[1]
                    pe.wait_ge(hm_ready, c + 1)
                    ps = take(s)
                    hm = HM[c % 4][:].rearrange("p h v -> p (h v)")
                    for j in range(ML_T):
                        one = T.transpose(ps[:, j * P:(j + 1) * P], hm[:, j * P:(j + 1) * P], IDN[:])
                    done(one, s)
                elif k == "YS":
                    pe.wait_ge(ld_y8, 16)
                    ps = take(s)
                    for j in range(ML_T):
                        one = T.transpose(ps[:, j * DEC:(j + 1) * DEC], HS8[:, j * P:(j + 1) * P], IDN[0:DEC, 0:DEC])
                    done(one, s)
                elif k == "POOL":
                    j = s[1]
                    u = N_MIX - LRU_T - POOL_T + j
                    pe.wait_ge((u_diff, u1_diff)[j], 2)
                    pe.wait_ge(u_small, j + 1)
                    for c in range(NCH):
                        key = (*s, c)
                        done(T.matmul(take(key)[:, 0:CH], BDP[:, j, :], ST[u % 2][:, c * CH:(c + 1) * CH], start=True, stop=True), key)

            def units(first, g, hi, lo, ready, paired=False, norm=None):
                for k in range(2 * NCH):
                    j, c, bank, v = (k % 2, k // 2, k % 3, k // 3) if paired else (k // 3, k % 3, k % 3, k // 3)
                    if k == 0 or k == (1 if paired else NCH):
                        pe.wait_ge(w_lo_ready, g * 2 + (first + j + 1))
                    pe.wait_ge(lo_ready, ready(c))
                    pe.wait_ge(d_free[bank], g * 2 + (first + v))
                    dense((first + j) % 2, c, hi, lo, bank)
                    if norm is not None and k in (2, 4, 5):
                        n, base = norm
                        done_c = (2, 4, 5).index(k)
                        sum_squares(("NORM", n, done_c), done_c, ss_done, base + NCH * (KT - 2) + 2 * (done_c + 1))

            def ff1(b, u, pairs):
                with pe.Fori(*pairs) as g:
                    units(u, b * KT + g, H_hi, H_lo, lambda c: P_MIX + norm_done(c))

            def ff2(b, u, p, pairs):
                with pe.Fori(*pairs) as g:
                    units(u, b * KT + g, Y_hi, Y_lo, lambda c: b * (2 * PER) + (p + NCH * (KT - 1) + c + 1))

            with pe.Fori(0, N_OUT // 2 - 1) as g:
                units(N_MIX, g, Y_hi, Y_lo, lambda c: P_MIX)
            units(N_MIX, N_OUT // 2 - 1, Y_hi, Y_lo, lambda c: P_MIX, paired=True, norm=(2, 0))
            units(U_FF, 0, H_hi, H_lo, lambda c: P_MIX + norm_done(c), paired=True)
            ff1(0, U_FF, (1, KT // 2))
            ff2(0, U_FF + KT, P_FF, (0, KT // 2))
            with pe.Fori(0, FF_BLOCKS - 2) as b:
                ff1(b, U_MID, (0, KT // 2))
                ff2(b, U_MID + KT, P_MID, (0, KT // 2))
            ff1(0, U_LAST, (0, KT // 2))
            ff2(0, U_LAST + KT, P_LAST, (0, KT // 2 - 1))
            units(U_LAST + KT, KT // 2 - 1, Y_hi, Y_lo, lambda c: P_LAST + NCH * (KT - 1) + c + 1, paired=True, norm=(3, N_SQ))


def kernel(**inputs):
    import concourse.bacc as bacc
    from concourse.bass_utils import run_bass_kernel_spmd

    a = {k: np.ascontiguousarray(v) for k, v in inputs.items()}
    f32 = np.float32

    def units(w):
        k, n = w.shape
        return w.reshape(k // P, P, n // P, P).transpose(2, 1, 0, 3).reshape(n // P, P, (k // P) * P)

    def tiles(v):
        return v.reshape(-1, P).T

    w_in = a["w_in"][0]
    cut = np.cumsum([384, 384, 384, 384, 384, 384, HEADS, HEADS, 256])
    xr, gr, q, k, v, o, ig, fg, u = np.split(w_in, cut[:-1], axis=1)
    wff2 = a["w_ff2"][0]
    ff1 = units(a["w_ff1"][0])
    mlp = []
    for b in range(FF_BLOCKS):
        mlp += [ff1[b * KT:(b + 1) * KT], units(wff2[b * D:(b + 1) * D])]
    W = np.concatenate([units(xr), units(k), units(q), units(o), units(u), units(gr), units(a["w_out"][0])] + mlp)
    wv = np.concatenate([v, ig, fg], axis=1).reshape(KT, P, VCOLS).transpose(1, 0, 2)
    conv_w = a["conv_w"][0].reshape(CONV, LRU_T, P).transpose(2, 1, 0).reshape(P, LRU_T * CONV)
    h0 = a["state_lru_h"][0].reshape(DEC, LRU_T, P).transpose(2, 1, 0).reshape(P, LRU_T * DEC)
    win = np.array(WINS).reshape(POOL_T, 2).repeat(64, axis=1)
    inv_win = (1.0 / win).T.astype(f32)
    t = np.arange(PBUF)
    fix = (win[:, :, None] / np.minimum(t + 1, win[:, :, None])).transpose(1, 0, 2).reshape(P, POOL_T * PBUF).astype(f32)
    cols = np.concatenate([tiles(a["norm1_g"][0]), tiles(a["norm2_g"][0]), tiles(a["final_g"]), tiles(a["b_ada"][0]), conv_w,
                           tiles(a["conv_b"][0]), tiles(a["lru_ba"][0].reshape(-1)), tiles(a["lru_bx"][0].reshape(-1)),
                           tiles(a["lru_lam"][0]), tiles(a["pool_scale"][0].reshape(-1)), inv_win,
                           tiles(a["mlstm_norm_g"][0].reshape(-1)), fix, h0], axis=1)
    bd = np.zeros((P, 2 * LRU_T + POOL_T, P), f32)
    for i in range(2 * LRU_T):
        t_, e = i // 2, i % 2
        bd[64 * e:64 * e + 64, t_, 64 * e:64 * e + 64] = a["lru_wa"][0, i]
        bd[64 * e:64 * e + 64, LRU_T + t_, 64 * e:64 * e + 64] = a["lru_wx"][0, i]
    for i in range(2 * POOL_T):
        t_, e = i // 2, i % 2
        bd[64 * e:64 * e + 64, 2 * LRU_T + t_, 64 * e:64 * e + 64] = a["pool_w"][0, i]
    conv_state = np.zeros((P, LRU_T, DEC, CONV), f32)
    conv_state[:, :, :, 0:CONV - 1] = a["state_lru_conv"][0].reshape(DEC, CONV - 1, LRU_T, P).transpose(3, 2, 0, 1)
    pool_buf = np.zeros((P, POOL_T, DEC, PBUF + 1), f32)
    pool_buf[:, :, :, 0:PBUF] = a["state_pool"][0].reshape(DEC, PBUF, POOL_T, P).transpose(3, 2, 0, 1)
    gate_bias = np.stack([a["mlstm_bi"][0].repeat(NLC + 1), a["mlstm_bf"][0].repeat(NLC + 1)], axis=1)
    m0 = np.zeros((HEADS, NLC + 1, DEC), f32)
    m0[:, NLC, :] = a["state_mlstm_m"][0].T
    i = np.arange(LC)
    mask = np.where(i[:, None] <= i[None, :], 0.0, NEG_BIG).astype(f32)
    arrays = {
        "x": np.concatenate([a["x_prompt"][0], a["x_sample"][:, 0]]).T,
        "c": np.concatenate([a["c_prompt"], a["c_sample"]]).reshape(DEC + 1, KT, P).transpose(2, 1, 0),
        "W": W, "WADA": units(a["w_ada"][0]), "wv": wv, "cols": cols, "ident": np.eye(P, dtype=f32),
        "bdl": bd[:, :2 * LRU_T], "bdp": bd[:, 2 * LRU_T:],
        "conv_state": conv_state, "pool_buf": pool_buf, "mask": mask, "gate_bias": gate_bias,
        "m0": m0.reshape(ROWS, DEC), "C": a["state_mlstm_C"][0].reshape(P, HD // 4, HD),
        "n": a["state_mlstm_n"][0].reshape(DEC * HEADS, HD),
    }
    outs = {"y": (D, TOK), "lru": (P, LRU_T, DEC + 1), "conv_p": (P, LRU_T, CONV - 1), "conv_s": (P, LRU_T, DEC, CONV),
            "pool_p": (P, POOL_T, PBUF), "pool_s": (P, POOL_T, DEC, PBUF + 1), "C_p": (HD, HEADS, HV), "m_p": (1, ROWS),
            "C_s": (P, HD // 4, HD), "n_s": (DEC * HEADS, HD), "m_s": (ROWS, DEC, 4)}

    nc = bacc.Bacc("TRN2", target_bir_lowering=False, num_devices=1, dynamic_dma_scratch_size=1024)
    arrays = {f"in_{n}": np.ascontiguousarray(v) for n, v in arrays.items()}
    I = {n[3:]: nc.dram_tensor(n, v.shape, mybir.dt.from_np(v.dtype), kind="ExternalInput").ap() for n, v in arrays.items()}
    O = {n: nc.dram_tensor(f"out_{n}", s, F32, kind="ExternalOutput").ap() for n, s in outs.items()}
    build(nc, I, O)
    r = run_bass_kernel_spmd(nc, [arrays], core_ids=[0]).results[0]
    g = {n: r[f"out_{n}"] for n in outs}
    y = g["y"].T
    lru = g["lru"].transpose(2, 1, 0).reshape(DEC + 1, LRU_T * P)
    m_p = g["m_p"].reshape(HEADS, NLC + 1)[:, NLC]
    C_p = g["C_p"].transpose(1, 2, 0)
    return (y[:SEQ][None], y[SEQ:][:, None],
            lru[0][None, None], g["conv_p"].transpose(2, 1, 0).reshape(1, 1, CONV - 1, LRU_T * P),
            C_p[:, :HD][None, None], C_p[:, HD][None, None], m_p[None, None],
            g["pool_p"].transpose(2, 1, 0).reshape(1, 1, PBUF, POOL_T * P),
            lru[1:][None], g["conv_s"][..., 1:].transpose(2, 3, 1, 0).reshape(1, DEC, CONV - 1, LRU_T * P),
            g["C_s"].reshape(1, DEC, HEADS, HD, HD), g["n_s"].reshape(1, DEC, HEADS, HD),
            g["m_s"].reshape(HEADS, NLC + 1, DEC, 4)[:, NLC, :, 3].T[None],
            g["pool_s"][..., 1:].transpose(2, 3, 1, 0).reshape(1, DEC, PBUF, POOL_T * P))
```
